# Optimizing a Trainium2 kernel written in Bass

```python
import math
import jax, jax.numpy as jnp
from jax import lax
import numpy as np

D_MODEL = 2048
BATCH = 1
SEQ = 256
DEPTH = 1
DEC_BATCH = 8
DEC_SEQ = 4
PAST_LEN = 2048
PAGE_SIZE = 128

D_MIX = D_MODEL
D_MLSTM = D_MIX // 2
N_HEADS = 4
HEAD_DIM = D_MLSTM // N_HEADS
D_CONV = D_MIX - D_MLSTM
CONV_WIDTH = 31
D_FF = 5632
CHUNK = 64
EPS = 1e-6
FFN_RES = 0.5
D_IN = 4 * D_MLSTM + 2 * D_CONV + 2 * N_HEADS

kernel_name = "hymba_mlstm_conformerconv_macaron_step"

def rmsnorm(x, g):
    xf = x.astype(jnp.float32)
    y = xf * lax.rsqrt(jnp.mean(xf * xf, axis=-1, keepdims=True) + EPS)
    return (y * g.astype(jnp.float32)).astype(x.dtype)

def layernorm(x, g, b):
    xf = x.astype(jnp.float32)
    mu = jnp.mean(xf, axis=-1, keepdims=True)
    var = jnp.mean(jnp.square(xf - mu), axis=-1, keepdims=True)
    y = (xf - mu) * lax.rsqrt(var + EPS)
    return (y * g.astype(jnp.float32) + b.astype(jnp.float32)).astype(x.dtype)

def swiglu(x, w_gate, w_up, w_down):
    return (jax.nn.silu(x @ w_gate) * (x @ w_up)) @ w_down

def mlstm_chunkwise(q, k, v, ig, lf, C0, n0, m0):
    B, T, H, Dh = q.shape
    L = math.gcd(T, CHUNK)
    nc = T // L

    def to_chunks(a):
        return jnp.moveaxis(a.reshape((B, nc, L) + a.shape[2:]), 1, 0)

    mask = jnp.tril(jnp.ones((L, L), dtype=bool))

    def step(carry, inp):
        C, n, m = carry
        qc, kc, vc, igc, lfc = inp
        bt = jnp.cumsum(lfc, axis=1).transpose(0, 2, 1)
        it = igc.transpose(0, 2, 1)
        D = bt[..., :, None] - bt[..., None, :] + it[..., None, :]
        D = jnp.where(mask, D, -jnp.inf)
        inter = bt + m[..., None]
        m_t = jnp.maximum(inter, jnp.max(D, axis=-1))
        w_intra = jnp.exp(D - m_t[..., None])
        w_inter = jnp.exp(inter - m_t)
        s = jnp.einsum('blhd,bshd->bhls', qc, kc) * w_intra
        num = (jnp.einsum('bhls,bshd->blhd', s, vc)
               + jnp.einsum('blhd,bhde->blhe', qc, C) * w_inter.transpose(0, 2, 1)[..., None])
        den = jnp.sum(s, axis=-1) + jnp.einsum('blhd,bhd->bhl', qc, n) * w_inter
        denom = jnp.maximum(jnp.abs(den), jnp.exp(-m_t))
        h = num / denom.transpose(0, 2, 1)[..., None]
        m_new = m_t[..., -1]
        g_state = jnp.exp(bt[..., -1] + m - m_new)
        g_keys = jnp.exp(bt[..., -1:] - bt + it - m_new[..., None])
        C_new = g_state[..., None, None] * C + jnp.einsum('bhs,bshd,bshe->bhde', g_keys, kc, vc)
        n_new = g_state[..., None] * n + jnp.einsum('bhs,bshd->bhd', g_keys, kc)
        return (C_new, n_new, m_new), h

    xs = (to_chunks(q), to_chunks(k), to_chunks(v), to_chunks(ig), to_chunks(lf))
    (C, n, m), hs = lax.scan(step, (C0, n0, m0), xs)
    h = jnp.moveaxis(hs, 0, 1).reshape(B, T, H, Dh)
    return h, C, n, m

def conformer_conv(a, b, conv_state, w_dw, b_dw, g_ln, b_ln):
    u = a * jax.nn.sigmoid(b)
    up = jnp.concatenate([conv_state.astype(u.dtype), u], axis=1)
    y = lax.conv_general_dilated(up, w_dw[:, None, :].astype(u.dtype), window_strides=(1,),
                                 padding='VALID', dimension_numbers=('NWC', 'WIO', 'NWC'),
                                 feature_group_count=D_CONV) + b_dw
    y = jax.nn.silu(layernorm(y, g_ln, b_ln))
    return y, up[:, -(CONV_WIDTH - 1):, :]

def layer(x, C0, n0, m0, conv0, p):
    B, T, _ = x.shape
    x = x + FFN_RES * rmsnorm(swiglu(rmsnorm(x, p['g_ffn1_pre']), p['w_ffn1_gate'], p['w_ffn1_up'],
                                     p['w_ffn1_down']), p['g_ffn1_post'])
    h = rmsnorm(x, p['g_mix_pre'])
    proj = h @ p['w_in']
    sizes = [D_MLSTM] * 4 + [D_CONV] * 2 + [N_HEADS] * 2
    cuts = np.cumsum(sizes)[:-1].tolist()
    q, k, v, o, ga, gb, ig, fg = jnp.split(proj, cuts, axis=-1)
    f32 = jnp.float32
    qh = q.astype(f32).reshape(B, T, N_HEADS, HEAD_DIM)
    kh = k.astype(f32).reshape(B, T, N_HEADS, HEAD_DIM) * (HEAD_DIM ** -0.5)
    vh = v.astype(f32).reshape(B, T, N_HEADS, HEAD_DIM)
    i_pre = ig.astype(f32) + p['b_igate'].astype(f32)
    log_f = jax.nn.log_sigmoid(fg.astype(f32) + p['b_fgate'].astype(f32))
    hm, C, n, m = mlstm_chunkwise(qh, kh, vh, i_pre, log_f, C0.astype(f32), n0.astype(f32), m0.astype(f32))
    hm = (jax.nn.sigmoid(o.astype(f32)) * hm.reshape(B, T, D_MLSTM)).astype(x.dtype)
    hc, conv_new = conformer_conv(ga, gb, conv0, p['w_dw'], p['b_dw'], p['g_conv_ln'], p['b_conv_ln'])
    mix = jnp.concatenate([hm, hc.astype(x.dtype)], axis=-1) @ p['w_out']
    x = x + rmsnorm(mix, p['g_mix_post'])
    x = x + FFN_RES * rmsnorm(swiglu(rmsnorm(x, p['g_ffn2_pre']), p['w_ffn2_gate'], p['w_ffn2_up'],
                                     p['w_ffn2_down']), p['g_ffn2_post'])
    return x, C, n, m, conv_new

def setup_inputs(seed: int = 0) -> dict:
    key = jax.random.key(seed)
    ks = iter(jax.random.split(key, 40))
    nrm = lambda shape, s: jax.random.normal(next(ks), shape, jnp.float32) * s
    gain = lambda shape: 1.0 + nrm(shape, 0.05)
    Lr = DEPTH
    b_f = jnp.broadcast_to(jnp.linspace(3.0, 6.0, N_HEADS, dtype=jnp.float32), (Lr, N_HEADS)) + nrm((Lr, N_HEADS), 0.01)
    return {
        "x_prompt": nrm((BATCH, SEQ, D_MODEL), 1.0),
        "x_sample": nrm((DEC_BATCH, DEC_SEQ, D_MODEL), 1.0),
        "state_mlstm_C": nrm((Lr, DEC_BATCH, N_HEADS, HEAD_DIM, HEAD_DIM), 0.1),
        "state_mlstm_n": nrm((Lr, DEC_BATCH, N_HEADS, HEAD_DIM), 0.1),
        "state_mlstm_m": nrm((Lr, DEC_BATCH, N_HEADS), 1.0),
        "state_conv": nrm((Lr, DEC_BATCH, CONV_WIDTH - 1, D_CONV), 0.5),
        "g_ffn1_pre": gain((Lr, D_MODEL)),
        "w_ffn1_gate": nrm((Lr, D_MODEL, D_FF), D_MODEL ** -0.5),
        "w_ffn1_up": nrm((Lr, D_MODEL, D_FF), D_MODEL ** -0.5),
        "w_ffn1_down": nrm((Lr, D_FF, D_MODEL), D_FF ** -0.5),
        "g_ffn1_post": gain((Lr, D_MODEL)),
        "g_mix_pre": gain((Lr, D_MODEL)),
        "w_in": nrm((Lr, D_MODEL, D_IN), D_MODEL ** -0.5),
        "b_igate": nrm((Lr, N_HEADS), 0.1),
        "b_fgate": b_f,
        "w_dw": nrm((Lr, CONV_WIDTH, D_CONV), CONV_WIDTH ** -0.5),
        "b_dw": nrm((Lr, D_CONV), 0.02),
        "g_conv_ln": gain((Lr, D_CONV)),
        "b_conv_ln": nrm((Lr, D_CONV), 0.02),
        "w_out": nrm((Lr, D_MIX, D_MODEL), D_MIX ** -0.5),
        "g_mix_post": gain((Lr, D_MODEL)),
        "g_ffn2_pre": gain((Lr, D_MODEL)),
        "w_ffn2_gate": nrm((Lr, D_MODEL, D_FF), D_MODEL ** -0.5),
        "w_ffn2_up": nrm((Lr, D_MODEL, D_FF), D_MODEL ** -0.5),
        "w_ffn2_down": nrm((Lr, D_FF, D_MODEL), D_FF ** -0.5),
        "g_ffn2_post": gain((Lr, D_MODEL)),
    }

def reference(x_prompt, x_sample, state_mlstm_C, state_mlstm_n, state_mlstm_m, state_conv,
              g_ffn1_pre, w_ffn1_gate, w_ffn1_up, w_ffn1_down, g_ffn1_post,
              g_mix_pre, w_in, b_igate, b_fgate, w_dw, b_dw, g_conv_ln, b_conv_ln, w_out, g_mix_post,
              g_ffn2_pre, w_ffn2_gate, w_ffn2_up, w_ffn2_down, g_ffn2_post):
    sdt = state_mlstm_C.dtype
    Bp = x_prompt.shape[0]
    xp, xs = x_prompt, x_sample
    Cp_l, np_l, mp_l, cp_l = [], [], [], []
    Cs_l, ns_l, ms_l, cs_l = [], [], [], []
    for l in range(DEPTH):
        p = {
            'g_ffn1_pre': g_ffn1_pre[l], 'w_ffn1_gate': w_ffn1_gate[l], 'w_ffn1_up': w_ffn1_up[l],
            'w_ffn1_down': w_ffn1_down[l], 'g_ffn1_post': g_ffn1_post[l],
            'g_mix_pre': g_mix_pre[l], 'w_in': w_in[l], 'b_igate': b_igate[l], 'b_fgate': b_fgate[l],
            'w_dw': w_dw[l], 'b_dw': b_dw[l], 'g_conv_ln': g_conv_ln[l], 'b_conv_ln': b_conv_ln[l],
            'w_out': w_out[l], 'g_mix_post': g_mix_post[l],
            'g_ffn2_pre': g_ffn2_pre[l], 'w_ffn2_gate': w_ffn2_gate[l], 'w_ffn2_up': w_ffn2_up[l],
            'w_ffn2_down': w_ffn2_down[l], 'g_ffn2_post': g_ffn2_post[l],
        }
        C0 = jnp.zeros((Bp, N_HEADS, HEAD_DIM, HEAD_DIM), jnp.float32)
        n0 = jnp.zeros((Bp, N_HEADS, HEAD_DIM), jnp.float32)
        m0 = jnp.zeros((Bp, N_HEADS), jnp.float32)
        conv0 = jnp.zeros((Bp, CONV_WIDTH - 1, D_CONV), xp.dtype)
        xp, Cp, npp, mp, cp = layer(xp, C0, n0, m0, conv0, p)
        xs, Cs, ns, ms, cs = layer(xs, state_mlstm_C[l], state_mlstm_n[l], state_mlstm_m[l], state_conv[l], p)
        Cp_l.append(Cp.astype(sdt)); np_l.append(npp.astype(sdt)); mp_l.append(mp.astype(sdt)); cp_l.append(cp.astype(sdt))
        Cs_l.append(Cs.astype(sdt)); ns_l.append(ns.astype(sdt)); ms_l.append(ms.astype(sdt)); cs_l.append(cs.astype(sdt))
    return (xp, xs,
            jnp.stack(Cp_l), jnp.stack(np_l), jnp.stack(mp_l), jnp.stack(cp_l),
            jnp.stack(Cs_l), jnp.stack(ns_l), jnp.stack(ms_l), jnp.stack(cs_l))


_drawn_inputs = setup_inputs


def setup_inputs(seed=0):
    import zlib

    import numpy as np

    out = dict(_drawn_inputs(seed))
    spreads = {}
    factors = {'b_dw': 3.473, 'b_conv_ln': 7.614, 'g_ffn2_post': 3.455}
    for name, (base, spread) in spreads.items():
        noise = np.random.default_rng([zlib.crc32(name.encode()), seed]).standard_normal(out[name].shape)
        drawn = base * np.exp(spread * noise) if base else spread * noise
        out[name] = __import__('jax').numpy.asarray(drawn.astype(out[name].dtype))
    for name, factor in factors.items():
        out[name] = (out[name] * factor).astype(out[name].dtype)
    return out
```

```python
from contextlib import ExitStack

import concourse.bass as bass
import concourse.mybir as mybir
import numpy as np

F32 = mybir.dt.float32
F32R = mybir.dt.float32r
ALU = mybir.AluOpType
ACT = mybir.ActivationFunctionType
AX_X = mybir.AxisListType.X

P = 128
D_MODEL = 2048
D_FF = 5632
SEQ = 256
NB, NT = 8, 4
NS = NB * NT
TOK = SEQ + NS
H, DH = 4, 256
DC = DH // P
D_MLSTM = H * DH
D_CONV = D_MODEL - D_MLSTM
TAPS = 31
HIST = TAPS - 1
EPS = 1e-6
XC = D_MODEL // P
CC = D_CONV // P
CH = 8
SLOTS = 4
PIECE = CH * P
FF_HALVES = (24, 20)
HEAD_TILES = 12
LOOK = 3

UP_PIECES = [2 * n * XC // CH for n in FF_HALVES]
DOWN_PIECES = [XC * n // CH for n in FF_HALVES]
FFN_PIECES = sum(UP_PIECES) + sum(DOWN_PIECES)
FFN_TILES = sum(2 * n + XC for n in FF_HALVES)
GATE_P, GATE_T = FFN_PIECES, FFN_TILES
HEAD_P, HEAD_T = GATE_P + XC // CH, GATE_T + 1
OUT_P, OUT_T = HEAD_P + H * HEAD_TILES * XC // CH, HEAD_T + H * HEAD_TILES
FFN2_P, FFN2_T = OUT_P + XC * XC // CH, OUT_T + XC
PIECES = FFN2_P + FFN_PIECES

GAINS = ("g_ffn1_pre", "g_ffn1_post", "g_mix_pre", "g_mix_post", "g_ffn2_pre", "g_ffn2_post")
V_TAP = len(GAINS) * XC
V_BDW = V_TAP + CC * TAPS
V_GLN = V_BDW + CC
V_BLN = V_GLN + CC
VEC = V_BLN + CC

R_BM, R_EM, R_GK, R_WI, ROWS = 0, TOK, 2 * TOK, 3 * TOK, 3 * TOK + NS
PADT = 1 + SEQ + NB * (1 + NT)
UP_W = HIST + SEQ + NB * (HIST + NT)
NEW_C = HIST * (1 + NB)


def at(base, per, i):
    return base if i is None else i * per + base


class Chain:

    def __init__(self, eng, sem):
        self.eng, self.sem, self.base, self.k, self.i, self.per = eng, sem, 0, 0, None, 0

    def link(self, ins):
        ins.then_inc(self.sem, 1)
        self.k += 1
        self.eng.wait_ge(self.sem, at(self.base + self.k, self.per, self.i))

    def enter(self, i, per):
        self.base, self.k, self.i, self.per = self.base + self.k, 0, i, per

    def leave(self, times):
        assert self.k == self.per, (self.k, self.per)
        self.base, self.k, self.i, self.per = self.base + self.per * times, 0, None, 0


def hybrid_layer_kernel(nc, stream, x_in, vecs, gate_vec, c_in, n_in, conv_in,
                        y_out, cp_out, np_out, cs_out, ns_out, m_out, conv_out):
    with ExitStack() as ctx:
        def sb(name, shape, dt=F32):
            return ctx.enter_context(nc.sbuf_tensor(name, shape, dt))

        def sem(name):
            return ctx.enter_context(nc.semaphore(name))

        x = sb("x_res", [P, XC, TOK])
        xh = sb("xh", [P, XC, TOK], F32R)
        raw = sb("raw", [P, SLOTS, PIECE])
        whi = sb("whi", [P, SLOTS, PIECE], F32R)
        wlo = sb("wlo", [P, SLOTS, PIECE], F32R)
        vec = sb("vec", [P, VEC])
        ones = sb("ones", [P, P])
        ident = sb("ident", [P, P])
        rstd = sb("rstd", [P, TOK])
        rpost = sb("rpost", [P, TOK])
        ssq = sb("ssq", [P, TOK])
        sq = sb("sq", [P, 2, TOK])
        scr = sb("scr", [P, 7, TOK])

        arena = [-(-nc.sbuf_base // 32) * 32]
        pad_bytes = -(-4 * PADT // 32) * 32

        def place(name, shape, dt=F32, where=None):
            t = nc.alloc_sbuf_tensor_at(name, shape, dt, offset=where if where is not None else arena[0])
            if where is None:
                arena[0] += -(-4 * int(np.prod(shape[1:])) // 32) * 32
            return t

        xl = place("xl", [P, XC, TOK], F32R)
        mix_at = arena[0]
        hh = place("hh", [P, FF_HALVES[0], TOK], F32R)
        hl = place("hl", [P, FF_HALVES[0], TOK], F32R)
        y_at = arena[0]
        y = place("y", [P, XC, TOK])
        y_end = arena[0]
        assert arena[0] <= nc.sbuf_usable_end, arena
        arena[0] = mix_at
        mh = place("mh", [P, D_MLSTM // P, TOK], F32R)
        ml = place("ml", [P, D_MLSTM // P, TOK], F32R)
        qkvo = place("qkvo", [P, 4, DC, TOK])
        yc = place("yc", [P, CC, TOK])
        c_at = arena[0]
        C = place("C", [P, NB, DC, DH])
        lfb = place("lfb", [H, PADT], F32, c_at)
        lfm = place("lfm", [H, PADT], F32, c_at + pad_bytes)
        igp = place("igp", [H, PADT], F32, c_at + 2 * pad_bytes)
        one = place("one", [H, PADT], F32, c_at + 3 * pad_bytes)
        bsum = place("bsum", [H, PADT], F32, c_at + 4 * pad_bytes)
        mrun = place("mrun", [H, PADT], F32, c_at + 5 * pad_bytes)
        cpr = place("cpr", [P, DC, DH])
        rows = place("rows", [H, ROWS])
        rowc = place("rowc", [H, TOK])
        bc = place("bc", [P, ROWS])
        vtok = place("vtok", [P, 2, DH])
        ktg = place("ktg", [P, 2, DH])
        vs = place("vs", [NS, DH])
        ksm = place("ksm", [NS, NB, DH])
        wt = place("wt", [P, SEQ + P + NS])
        ks = place("ks", [NS, DH], F32, arena[0])
        st = place("st", [P, SEQ + P + NS])
        upad = place("upad", [P, 2, UP_W])
        hist = place("hist", [P, 2, NB * HIST])
        newc = place("newc", [P, 2, NEW_C])
        wcur = place("wcur", [P, 2, TAPS])
        bcur = place("bcur", [P, 2])
        ysum = sq[:, 0, :]
        sel = place("sel", [H, P])
        colc = place("colc", [P, 4])
        cols = place("cols", [NS, 2])
        gkm = place("gkm", [NS, NB])
        mask = place("mask", [NS, NB])
        gv = place("gv", [H, 2 + NB])
        n0 = place("n0", [P, H, DC, NB])
        nns = place("nns", [P, H, DC, NB])
        nnp = place("nnp", [P, H, DC])
        nred = place("nred", [P, DC, NB])
        qw = place("qw", [P, DC, NS])
        qwn = place("qwn", [P, DC, NS])
        qcs = place("qcs", [P, DC, NS])
        mout = place("mout", [H, 1 + NB])
        assert arena[0] <= nc.sbuf_usable_end, (arena, nc.sbuf_usable_end)
        sq8 = qkvo[:, :, :, :].rearrange("p a b t -> p (a b) t")
        sg8 = C[:, :, :, :].rearrange("p b c e -> p (b c e)")[:, 0:CC * TOK].rearrange("p (c t) -> p c t", c=CC)

        bank = [ctx.enter_context(nc.psum_tensor(f"bank{i}", [P, 512], F32)) for i in range(8)]

        landed = [sem(f"piece_landed{s}") for s in range(SLOTS)]
        x_landed = [sem(f"x_landed{c}") for c in range(4)]
        vec_landed, small_landed = sem("vec_landed"), sem("small_landed")
        hi_ready = sem("hi_ready")
        lo_ready = [sem("lo_ready_even"), sem("lo_ready_odd")]
        piece_done = sem("piece_done")
        tile_evicted = sem("tile_evicted")
        consts_ready = sem("consts_ready")
        x_hi, x_ready, x_new = sem("x_hi"), sem("x_ready"), sem("x_new")
        sq_ready, ssq_added, ssq_clear = sem("sq_ready"), sem("ssq_added"), sem("ssq_clear")
        norm_sum, norm_var, norm_sd = sem("norm_sum"), sem("norm_var"), sem("norm_sd")
        sig_ready, gated, h_f32, h_hi, h_ready = (sem("sig_ready"), sem("gated"), sem("h_f32"),
                                                  sem("h_hi"), sem("h_ready"))
        dve_chain, act_chain, pool_chain = sem("dve_chain"), sem("act_chain"), sem("pool_chain")
        pads_ready, az_ready, e_ready, e1_ready, ln_ready = (sem("pads_ready"), sem("az_ready"), sem("e_ready"),
                                                             sem("e1_ready"), sem("ln_ready"))
        args_ready, rows_ready, m_ready = sem("args_ready"), sem("rows_ready"), sem("m_ready")
        sel_ready, rowsT_done, bc_ready, col_ready = (sem("sel_ready"), sem("rowsT_done"), sem("bc_ready"),
                                                      sem("col_ready"))
        hist_landed, hist_ready, sigb_ready, u_ready = (sem("hist_landed"), sem("hist_ready"),
                                                        sem("sigb_ready"), sem("u_ready"))
        newc_ready, conv_done, ysum_added = sem("newc_ready"), sem("conv_done"), sem("ysum_added")
        w_exp, w_ready = sem("w_exp"), sem("w_ready")
        tr_done, tr_evicted, ksm_ready, qw_ready = (sem("tr_done"), sem("tr_evicted"), sem("ksm_ready"),
                                                    sem("qw_ready"))
        qc_done, qc_evicted, cu_done, cu_evicted = (sem("qc_done"), sem("qc_evicted"), sem("cu_done"),
                                                    sem("cu_evicted"))
        sc_done, st_ready, num_done, hm_num = sem("sc_done"), sem("st_ready"), sem("num_done"), sem("hm_num")
        osig_ready, hm_ready, hm_hi, mix_ready, kg_ready, kg_read = (
            sem("osig_ready"), sem("hm_ready"), sem("hm_hi"), sem("mix_ready"), sem("kg_ready"), sem("kg_read"))
        c_landed, stored, out_stored, small_stored = (sem("c_landed"), sem("c_stored"), sem("out_stored"),
                                                      sem("small_stored"))
        ln_sum, ln_mu, ln_cent, ln_sq, ln_sqsum, ln_var, ln_sd = (
            sem("ln_sum"), sem("ln_mu"), sem("ln_cent"), sem("ln_sq"), sem("ln_sqsum"), sem("ln_var"), sem("ln_sd"))
        ln_yn, ln_z, ln_sig, ln_silu, ln_hi, conv_ready = (
            sem("ln_yn"), sem("ln_z"), sem("ln_sig"), sem("ln_silu"), sem("ln_hi"), sem("conv_ready"))
        nn_ready = sem("nn_ready")

        block = ctx.enter_context(nc.Block())

        def gain(name, c):
            k = GAINS.index(name) * XC + c
            return vec[:, k:k + 1]

        def padded(row, k):
            if k == 0:
                return row[:, 1:1 + SEQ]
            return row[:, 1 + SEQ:PADT].rearrange("h (b t) -> h b t", b=NB)[:, :, 1:1 + NT]

        def resets(row):
            return row[:, 1 + SEQ:PADT].rearrange("h (b t) -> h b t", b=NB)[:, :, 0:1]

        def compact(row, k):
            if k == 0:
                return row[:, 0:SEQ]
            return row[:, SEQ:TOK].rearrange("h (b t) -> h b t", b=NB)

        def up_prompt(j, n, off=0):
            return upad[:, j, off:off + n]

        def up_dec(j, n, off=0):
            return upad[:, j, HIST + SEQ:UP_W].rearrange("p (b w) -> p b w", b=NB)[:, :, off:off + n]

        @block.sync
        def _(sp):
            sp.dma_start(vec[:, :], vecs).then_inc(vec_landed, 16)
            for c in range(0, XC, 4):
                sp.dma_start(x[:, c:c + 4, :], x_in[:, c:c + 4, :]).then_inc(x_landed[c // 4], 16)
            for g in range(SLOTS):
                sp.dma_start(raw[:, g, :], stream[g]).then_inc(landed[g], 16)
            with sp.Fori(1, PIECES // SLOTS) as m:
                for s in range(SLOTS):
                    sp.wait_ge(lo_ready[s % 2], m * 2 + (s // 2 - 1))
                    sp.dma_start(raw[:, s, :], stream[m * SLOTS + s]).then_inc(landed[s], 16)
            for g in range(PIECES // SLOTS * SLOTS, PIECES):
                sp.wait_ge(lo_ready[g % 2], g // 2 - 1)
                sp.dma_start(raw[:, g % SLOTS, :], stream[g]).then_inc(landed[g % SLOTS], 16)
            for c in range(0, XC, 4):
                sp.wait_ge(x_new, 2 * XC + c + 4)
                sp.dma_start(y_out[:, c:c + 4, :], x[:, c:c + 4, :]).then_inc(out_stored, 16)
            sp.wait_ge(out_stored, 16 * (XC // 4))
            sp.wait_ge(stored, 32 + 48 * H)
            sp.wait_ge(small_stored, 32)

        @block.tensor
        def _(pe):
            def tile_start(T, per, i):
                if i is not None or T >= 4:
                    pe.wait_ge(tile_evicted, at(T - 3, per, i))

            def piece_start(g, per, i):
                pe.wait_ge(lo_ready[g % 2], at(g // 2 + 1, per // 2, i))

            def multiply(T, g, j, k, mov_hi, mov_lo, first, last):
                out = bank[T % 4][:, 0:TOK]
                wh = whi[:, g % SLOTS, j * P:(j + 1) * P]
                wl = wlo[:, g % SLOTS, j * P:(j + 1) * P]
                pe.matmul(out, wh, mov_hi[:, k, :], start=first, stop=False)
                pe.matmul(out, wh, mov_lo[:, k, :], start=False, stop=False)
                return pe.matmul(out, wl, mov_hi[:, k, :], start=False, stop=last)

            def project(T, g, tper, gper, i, x_from=None):
                tile_start(T, tper, i)
                for n in range(XC // CH):
                    piece_start(g + n, gper, i)
                    for j in range(CH):
                        k = n * CH + j
                        if x_from is not None:
                            pe.wait_ge(x_ready, x_from + k + 1)
                        last = multiply(T, g + n, j, k, xh, xl, k == 0, k == XC - 1)
                    last.then_inc(piece_done, 1)

            def column_sums(n, out, src):
                pe.matmul(out, ones[:, :], src, start=True, stop=True).then_inc(norm_sum, 1)

            def down(T, g, per_tile, tiles, n_chunks, tper, gper, i, h_from):
                for f in range(tiles * n_chunks):
                    t, k = divmod(f, n_chunks)
                    if k == 0:
                        tile_start(T + t, tper, i)
                    if f % CH == 0:
                        piece_start(g + f // CH, gper, i)
                        pe.wait_ge(h_ready, h_from + min(n_chunks, k + CH))
                    last = multiply(T + t, g + f // CH, f % CH, k, hh, hl, k == 0, k == n_chunks - 1)
                    if f % CH == CH - 1:
                        last.then_inc(piece_done, 1)

            def ffn(g, T, h_from, x_from, norm_at):
                for half, n in enumerate(FF_HALVES):
                    start = 0
                    if half == 0:
                        for q in range(4):
                            project(T + q, g + 2 * q, 0, 0, None, x_from if q == 0 else None)
                            if q == 0:
                                pe.wait_ge(ssq_added, norm_at)
                                column_sums(0, bank[4][:, 0:TOK], ssq[:, :])
                        start = 1
                    with pe.Fori(start, n // 2) as i:
                        for q in range(4):
                            project(T + q, g + 2 * q, 4, 8, i)
                    T, g = T + 2 * n, g + UP_PIECES[half]
                    tiles = 4 if half == 0 else 8
                    with pe.Fori(0, XC // tiles) as i:
                        down(T, g, 0, tiles, n, tiles, tiles * n // CH, i, h_from)
                    T, g, h_from = T + XC, g + DOWN_PIECES[half], h_from + n
                return g, T

            pe.wait_ge(consts_ready, 1)
            ffn(0, 0, 0, 0, XC)
            pe.wait_ge(ssq_added, 2 * XC)
            column_sums(1, bank[4][:, 0:TOK], ssq[:, :])

            project(GATE_T, GATE_P, 0, 0, None, XC)
            pe.wait_ge(ssq_added, 3 * XC)
            column_sums(2, bank[4][:, 0:TOK], ssq[:, :])

            def broadcast_rows(h):
                pe.wait_ge(args_ready, 1)
                pe.wait_ge(rows_ready, 4)
                pe.wait_ge(sel_ready, at(1, 1, h))
                pe.wait_ge(tile_evicted, at(HEAD_T + 1, HEAD_TILES, h))
                pe.wait_ge(norm_var, 3)
                half = ROWS // 2
                pe.matmul(bank[5][:, 0:half], sel[:, :], rows[:, 0:half], start=True, stop=True).then_inc(rowsT_done, 1)
                pe.matmul(bank[6][:, 0:half], sel[:, :], rows[:, half:ROWS], start=True, stop=True).then_inc(rowsT_done, 1)
                I4 = ident[0:H, 0:H]
                for t in range(2):
                    pe.transpose(bank[4][:, 4 * t:4 * t + 4], rowc[:, t * P:(t + 1) * P], I4)
                    pe.transpose(bank[4][:, 8 + 4 * t:12 + 4 * t], rows[:, R_GK + t * P:R_GK + (t + 1) * P], I4)
                pe.transpose(bank[4][0:NS, 16:20], rowc[:, SEQ:TOK], I4)
                pe.transpose(bank[4][0:NS, 20:24], rows[:, R_GK + SEQ:R_GK + TOK], I4).then_inc(rowsT_done, 1)

            def to_token_major(h):
                pe.wait_ge(tile_evicted, at(HEAD_T + 8, HEAD_TILES, h))
                for j, src in enumerate((2, 1)):
                    for c in range(DC):
                        mm = pe.transpose(bank[7][0:NS, (2 * j + c) * P:(2 * j + c + 1) * P],
                                          qkvo[:, src, c, SEQ:TOK], ident[:, :])
                mm.then_inc(tr_done, 1)
                pe.wait_ge(bc_ready, at(2, 2, h))
                for b, src in ((5, 2), (6, 1)):
                    for t in range(2):
                        for c in range(DC):
                            mm = pe.transpose(bank[b][:, (2 * t + c) * P:(2 * t + c + 1) * P],
                                              qkvo[:, src, c, t * P:(t + 1) * P], ident[:, :])
                    mm.then_inc(tr_done, 1)

            def query_memory(h):
                pe.wait_ge(c_landed, at(16, 16, h))
                pe.wait_ge(qw_ready, at(1, 1, h))
                pe.wait_ge(tr_evicted, at(3, 3, h))
                for e in range(DC):
                    for b in range(NB):
                        for c in range(DC):
                            mm = pe.matmul(bank[7][:, e * NS + b * NT:e * NS + (b + 1) * NT],
                                           C[:, b, c, e * P:(e + 1) * P], qw[:, c, b * NT:(b + 1) * NT],
                                           start=(c == 0), stop=(c == DC - 1))
                mm.then_inc(qc_done, 1)

            def update_memory(h):
                pe.wait_ge(ksm_ready, at(1, 1, h))
                for b in range(NB + 1):
                    if b >= 2:
                        pe.wait_ge(cu_evicted, at(b - 1, NB + 1, h))
                    out = bank[5 + b % 2]
                    for c in range(DC):
                        if b < NB:
                            mm = pe.matmul(out[:, c * DH:(c + 1) * DH], ksm[:, b, c * P:(c + 1) * P], vs[:, :],
                                           start=True, stop=True)
                        else:
                            for t in range(2):
                                mm = pe.matmul(out[:, c * DH:(c + 1) * DH], ktg[:, t, c * P:(c + 1) * P],
                                               vtok[:, t, :], start=(t == 0), stop=(t == 1))
                    mm.then_inc(cu_done, 1)

            def scores(h):
                pe.wait_ge(col_ready, at(1, 1, h))
                k, q = qkvo[:, 1, :, :], qkvo[:, 0, :, :]
                for lo, n, s, m, l in ((0, SEQ, 0, P, 0), (SEQ, P, P, P, P), (SEQ + P, NS, SEQ, NS, SEQ)):
                    for c in range(DC):
                        mm = pe.matmul(bank[4][0:m, lo:lo + n], k[:, c, s:s + m], q[:, c, l:l + n],
                                       start=(c == 0), stop=(c == DC - 1))
                mm.then_inc(sc_done, 1)

            def attend(h):
                pe.wait_ge(st_ready, at(1, 1, h))
                pe.wait_ge(qc_evicted, at(1, 1, h))
                out = bank[7]
                pe.matmul(out[:, 0:SEQ], ones[:, :], st[:, 0:SEQ], start=True, stop=False, skip_group_check=True)
                pe.matmul(out[:, P:SEQ], ones[:, :], st[:, SEQ:SEQ + P], start=False, stop=True, skip_group_check=True)
                pe.matmul(out[:, SEQ:TOK], ones[0:NS, :], st[0:NS, SEQ + P:SEQ + P + NS],
                          start=False, stop=False, skip_group_check=True)
                for c in range(DC):
                    mm = pe.matmul(out[:, SEQ:TOK], ones[:, :], qwn[:, c, :], start=False, stop=(c == DC - 1),
                                   skip_group_check=True)
                mm.then_inc(num_done, 1)
                pe.wait_ge(cu_evicted, at(NB + 1, NB + 1, h))
                for e in range(DC):
                    out = bank[5 + e]
                    pe.matmul(out[:, 0:SEQ], vtok[:, 0, e * P:(e + 1) * P], st[:, 0:SEQ], start=True, stop=False,
                              skip_group_check=True)
                    pe.matmul(out[:, P:SEQ], vtok[:, 1, e * P:(e + 1) * P], st[:, SEQ:SEQ + P], start=False,
                              stop=True, skip_group_check=True)
                    pe.matmul(out[:, SEQ:TOK], vs[:, e * P:(e + 1) * P], st[0:NS, SEQ + P:SEQ + P + NS],
                              start=False, stop=True, skip_group_check=True).then_inc(num_done, 1)

            with pe.Fori(0, H) as h:
                for q in range(HEAD_TILES):
                    project(HEAD_T + q, HEAD_P + 2 * q, HEAD_TILES, 2 * HEAD_TILES, h)
                    if q == 4:
                        broadcast_rows(h)
                    if q == 8:
                        to_token_major(h)
                    if q == 10:
                        query_memory(h)
                        update_memory(h)
                        scores(h)
                    if q == 11:
                        attend(h)

            def out_half(T, g, q, lo, i, conv_from=None):
                piece_start(g, 8, i)
                for j in range(CH):
                    if lo:
                        if conv_from is not None:
                            pe.wait_ge(conv_ready, conv_from + j + 1)
                        last = multiply_conv(T, g, j)
                    else:
                        last = multiply(T, g, j, j, mh, ml, j == 0, False)
                last.then_inc(piece_done, 1)

            def multiply_conv(T, g, j):
                out = bank[T % 4][:, 0:TOK]
                wh = whi[:, g % SLOTS, j * P:(j + 1) * P]
                wl = wlo[:, g % SLOTS, j * P:(j + 1) * P]
                pe.matmul(out, wh, xh[:, j, :], start=False, stop=False)
                pe.matmul(out, wh, xh[:, CC + j, :], start=False, stop=False)
                return pe.matmul(out, wl, xh[:, j, :], start=False, stop=(j == CH - 1))

            pe.wait_ge(ysum_added, 2 * H)
            pe.wait_ge(st_ready, H)
            pe.matmul(bank[4][:, 0:TOK], ones[:, :], ysum, start=True, stop=True).then_inc(ln_sum, 1)
            pe.wait_ge(mix_ready, 2 * H)
            for q in range(4):
                tile_start(OUT_T + q, 0, None)
                out_half(OUT_T + q, OUT_P + q, q, False, None)
                if q == 0:
                    pe.wait_ge(hm_num, 3 * H)
                    for c in range(CC):
                        pe.wait_ge(ln_sq, c + 1)
                        mm = pe.matmul(bank[5][:, 0:TOK], ones[:, :], sq8[:, c, :], start=(c == 0), stop=(c == CC - 1))
                    mm.then_inc(ln_sqsum, 1)
            for q in range(4):
                out_half(OUT_T + q, OUT_P + 4 + q, q, True, None, 0 if q == 0 else None)
            with pe.Fori(1, XC // 4) as i:
                for q in range(4):
                    tile_start(OUT_T + q, 4, i)
                    out_half(OUT_T + q, OUT_P + q, q, False, i)
                for q in range(4):
                    out_half(OUT_T + q, OUT_P + 4 + q, q, True, i)
            pe.wait_ge(ssq_added, 4 * XC)
            column_sums(3, bank[4][:, 0:TOK], ssq[:, :])
            ffn(FFN2_P, FFN2_T, sum(FF_HALVES), 2 * XC, 5 * XC)
            pe.wait_ge(ssq_added, 6 * XC)
            column_sums(5, bank[4][:, 0:TOK], ssq[:, :])

        @block.scalar
        def _(act):
            def split_hi(g, per=0, i=None):
                if g >= PIECES:
                    return
                act.wait_ge(landed[g % SLOTS], at(16 * (g // SLOTS + 1), 16 * per // SLOTS, i))
                if g >= SLOTS or i is not None:
                    act.wait_ge(piece_done, at(g - 3, per, i))
                act.activation(whi[:, g % SLOTS, :], raw[:, g % SLOTS, :], ACT.Copy).then_inc(hi_ready, 1)

            def square(src, n):
                if n >= 2:
                    act.wait_ge(ssq_added, n - 1)
                act.activation(sq[:, n % 2, :], src, ACT.Square).then_inc(sq_ready, 1)

            def norm_root(k, scale):
                act.wait_ge(norm_var, k + 1)
                act.activation(scr[:, 6, :], scr[:, 5, :], ACT.Sqrt, scale=scale).then_inc(norm_sd, 1)

            def x_operands(pre, n_new, n_sq):
                for c in range(XC):
                    if n_new is None:
                        act.wait_ge(x_landed[c // 4], 16)
                    else:
                        act.wait_ge(x_new, n_new + c + 1)
                    act.activation(xh[:, c, :], x[:, c, :], ACT.Copy, scale=gain(pre, c)).then_inc(x_hi, 1)
                    square(x[:, c, :], n_sq + c)

            def ffn(g, T, f_from, sq_from, norm_at):
                for half, n in enumerate(FF_HALVES):
                    def body(i, first):
                        for jj in range(2):
                            f = f_from + jj
                            split_hi(g + 4 * jj + 3, 8, i)
                            split_hi(g + 4 * jj + 4, 8, i)
                            if first and jj == 0:
                                norm_root(norm_at, 1.0)
                            act.wait_ge(tile_evicted, at(T + 2 * jj + 1, 4, i))
                            if i is not None or f >= 1:
                                act.wait_ge(gated, at(f, 2, i))
                            act.activation(scr[:, 2, :], scr[:, jj, :], ACT.Sigmoid).then_inc(sig_ready, 1)
                            split_hi(g + 4 * jj + 5, 8, i)
                            split_hi(g + 4 * jj + 6, 8, i)
                            act.wait_ge(h_f32, at(f + 1, 2, i))
                            act.activation(hh[:, jj if i is None else i * 2 + jj, :], scr[:, 4, :], ACT.Copy)\
                               .then_inc(h_hi, 1)

                    if half == 0:
                        body(None, True)
                    with act.Fori(1 - half, n // 2) as i:
                        body(i, False)
                    T, g = T + 2 * n, g + UP_PIECES[half]
                    tiles = 4 if half == 0 else 8
                    per = tiles * n // CH
                    loops = XC // tiles
                    last = g + per * loops == PIECES
                    with act.Fori(0, loops - last) as i:
                        down_body(g, T, tiles, n, per, i, half, sq_from, 0)
                    if last:
                        d = tiles * (loops - 1)
                        down_body(g + per * (loops - 1), T + d, tiles, n, per, None, half, sq_from + d, d)
                    T, g, f_from = T + XC, g + DOWN_PIECES[half], f_from + n

            def down_body(g, T, tiles, n, per, i, half, sq_from, d0):
                t = 0
                for p in range(per):
                    split_hi(g + p + LOOK, per, i)
                    if (p + 1) * CH >= (t + 1) * n:
                        if half == 1:
                            act.wait_ge(tile_evicted, at(T + t + 1, tiles, i))
                            act.wait_ge(ssq_added, at(sq_from + t - 1, tiles, i))
                            act.activation(sq[:, (sq_from + t) % 2, :], y[:, at(d0 + t, tiles, i), :],
                                           ACT.Square).then_inc(sq_ready, 1)
                        t += 1

            act.wait_ge(vec_landed, 16)
            for g in range(LOOK):
                split_hi(g)
            x_operands("g_ffn1_pre", None, 0)
            ffn(0, 0, 0, XC, 0)
            norm_root(1, 4.0)
            x_operands("g_mix_pre", 0, 2 * XC)
            split_hi(GATE_P + 3)
            norm_root(2, 1.0)

            split_hi(GATE_P + 4)
            act.wait_ge(az_ready, 1)
            act.activation(scr[0:H, 3, :], scr[0:H, 2, :], ACT.Exp, scale=-1.0).then_inc(e_ready, 1)
            act.wait_ge(e1_ready, 1)
            act.activation(scr[0:H, 4, :], scr[0:H, 3, :], ACT.Ln).then_inc(ln_ready, 1)
            act.wait_ge(args_ready, 1)
            for k in range(2):
                act.activation(compact(rows[:, R_EM:R_EM + TOK], k), padded(mrun, k), ACT.Exp, scale=-1.0)\
                   .then_inc(rows_ready, 1)
            act.activation(rows[:, R_GK:R_GK + TOK], scr[0:H, 6, :], ACT.Exp).then_inc(rows_ready, 1)
            act.activation(rows[:, R_WI:ROWS], scr[0:H, 0, 0:NS], ACT.Exp).then_inc(rows_ready, 1)

            act.wait_ge(m_ready, 1)
            act.dma_start(m_out[:, 0:NT], mout[:, 0:NT]).then_inc(stored, 16)
            act.dma_start(m_out[:, NT:1 + NB], mout[:, NT:1 + NB]).then_inc(stored, 16)

            with act.Fori(0, H) as h:
                for q in range(HEAD_TILES):
                    split_hi(HEAD_P + 2 * q + 3, 2 * HEAD_TILES, h)
                    split_hi(HEAD_P + 2 * q + 4, 2 * HEAD_TILES, h)
                    if q == 0:
                        act.wait_ge(hi_ready, at(HEAD_P + 5, 2 * HEAD_TILES, h))
                        act.dma_start(hist[:, :, :], conv_in[h]).then_inc(hist_landed, 16)
                    if q in (1, 3):
                        act.wait_ge(tile_evicted, at(HEAD_T + q + 1, HEAD_TILES, h))
                        act.activation(scr[:, 2, :], scr[:, 1, :], ACT.Sigmoid).then_inc(sigb_ready, 1)
                    if q == 1:
                        act.wait_ge(hist_landed, at(16, 16, h))
                        for j in range(2):
                            act.activation(up_dec(j, HIST), hist[:, j, :].rearrange("p (b w) -> p b w", b=NB),
                                           ACT.Copy).then_inc(hist_ready, 1)
                    if q in (2, 4):
                        j = q // 2 - 1
                        act.wait_ge(u_ready, at(j + 1, 2, h))
                        act.wait_ge(stored, at(32, 48, h))
                        act.activation(newc[:, j, 0:HIST], up_prompt(j, HIST, SEQ), ACT.Copy)
                        act.activation(newc[:, j, HIST:NEW_C].rearrange("p (b w) -> p b w", b=NB),
                                       up_dec(j, HIST, NT), ACT.Copy).then_inc(newc_ready, 1)
                    if q == 3:
                        act.dma_start(C[:, :, :, :], c_in[h]).then_inc(c_landed, 16)
                    if q == 4:
                        act.wait_ge(newc_ready, at(2, 2, h))
                        act.dma_start(conv_out[h], newc[:, :, :]).then_inc(stored, 16)
                        for k in range(2):
                            act.wait_ge(rowsT_done, at(k + 1, 3, h))
                            half = ROWS // 2
                            act.activation(bc[:, k * half:(k + 1) * half], bank[5 + k][:, 0:half], ACT.Copy)\
                               .then_inc(bc_ready, 1)
                    if q == 5:
                        act.wait_ge(bc_ready, at(2, 2, h))
                        act.wait_ge(col_ready, at(1, 1, h))
                        act.activation(wt[:, 0:SEQ], bc[:, R_BM:R_BM + SEQ], ACT.Exp, bias=colc[:, 0:1])
                        act.activation(wt[:, SEQ:SEQ + P], bc[:, R_BM + P:R_BM + SEQ], ACT.Exp, bias=colc[:, 1:2])
                        act.activation(wt[0:NS, SEQ + P:SEQ + P + NS], bc[0:NS, R_BM + SEQ:R_BM + TOK], ACT.Exp,
                                       bias=cols[:, 0:1]).then_inc(w_exp, 1)
                    if q in (10, 11):
                        o = q - 10
                        act.wait_ge(tile_evicted, at(HEAD_T + q + 1, HEAD_TILES, h))
                        act.activation(qkvo[:, 3, o, :], scr[:, o, :], ACT.Sigmoid).then_inc(osig_ready, 1)
                    if q == 11:
                        for e in range(DC):
                            act.wait_ge(hm_ready, at(e + 1, 2, h))
                            act.activation(mh[:, h * DC + e, :], scr[:, 4 + e, :], ACT.Copy).then_inc(hm_hi, 1)
                        act.wait_ge(cu_evicted, at(NB + 1, NB + 1, h))
                        act.dma_start(cs_out[h], C[:, :, :, :]).then_inc(stored, 16)
                        act.dma_start(cp_out[h], cpr[:, :, :]).then_inc(stored, 16)

            split_hi(OUT_P + 3)
            for c in range(CC):
                act.wait_ge(ln_cent, c + 1)
                act.activation(sq8[:, c, :], yc[:, c, :], ACT.Square).then_inc(ln_sq, 1)
            act.wait_ge(ln_var, 1)
            act.activation(scr[:, 6, :], scr[:, 5, :], ACT.Sqrt).then_inc(ln_sd, 1)
            act.wait_ge(stored, 32 + 48 * H)
            for c in range(CC):
                if c == 4:
                    split_hi(OUT_P + 4)
                act.wait_ge(ln_yn, c + 1)
                act.activation(sg8[:, c, :], yc[:, c, :], ACT.Sigmoid, scale=vec[:, V_GLN + c:V_GLN + c + 1],
                               bias=vec[:, V_BLN + c:V_BLN + c + 1]).then_inc(ln_sig, 1)
            for c in range(CC):
                act.wait_ge(ln_silu, c + 1)
                act.activation(xh[:, c, :], yc[:, c, :], ACT.Copy).then_inc(ln_hi, 1)
            for p in range(5, 7):
                split_hi(OUT_P + p)

            def out_body(i, i0):
                for p in range(8):
                    if i is not None or p >= 4:
                        split_hi(OUT_P + p + LOOK + 8 * i0, 8, i)
                    if p >= 4:
                        t = p - 4
                        act.wait_ge(tile_evicted, at(OUT_T + t + 1 + 4 * i0, 4, i))
                        n = 3 * XC + t + 4 * i0
                        act.wait_ge(ssq_added, at(n - 1, 4, i))
                        act.activation(sq[:, n % 2, :], y[:, at(t + 4 * i0, 4, i), :], ACT.Square).then_inc(sq_ready, 1)

            out_body(None, 0)
            with act.Fori(1, XC // 4) as i:
                out_body(i, 0)
            norm_root(3, 1.0)
            x_operands("g_ffn2_pre", XC, 4 * XC)
            ffn(FFN2_P, FFN2_T, sum(FF_HALVES), 5 * XC, 4)
            norm_root(5, 4.0)

        @block.vector
        def _(dve):
            chain = Chain(dve, dve_chain)
            link = chain.link

            def split_lo(g, per=0, i=None):
                if g % 2 or g >= PIECES:
                    return
                dve.wait_ge(hi_ready, at(g + 1, per, i))
                dve.tensor_tensor(wlo[:, g % SLOTS, :], raw[:, g % SLOTS, :], whi[:, g % SLOTS, :].bitcast(F32),
                                  ALU.subtract).then_inc(lo_ready[0], 1)

            def norm_factor(k, out):
                dve.wait_ge(norm_sum, k + 1)
                dve.tensor_scalar(scr[:, 5, :], bank[4][:, 0:TOK], 1.0 / D_MODEL, EPS, ALU.mult, ALU.add)\
                   .then_inc(norm_var, 1)
                dve.wait_ge(norm_sd, k + 1)
                link(dve.reciprocal(out[:, :], scr[:, 6, :]))

            def x_lo(pre, c, n_x):
                dve.wait_ge(x_hi, n_x + c + 1)
                dve.scalar_tensor_tensor(out=xl[:, c, :], in0=x[:, c, :], scalar=gain(pre, c),
                                         in1=xh[:, c, :].bitcast(F32), op0=ALU.mult, op1=ALU.subtract)\
                   .then_inc(x_ready, 1)

            def residual(post, pre, n_x, n_new):
                for c in range(XC + 1):
                    if c < XC:
                        link(dve.tensor_tensor(scr[:, c % 2, :], y[:, c, :], rpost[:, :], ALU.mult))
                        dve.scalar_tensor_tensor(out=x[:, c, :], in0=scr[:, c % 2, :], scalar=gain(post, c),
                                                 in1=x[:, c, :], op0=ALU.mult, op1=ALU.add).then_inc(x_new, 1)
                    if c and pre:
                        x_lo(pre, c - 1, n_x)

            def evict_scaled(T, tper, i, out, k=None):
                src = bank[T % 4][:, 0:TOK]
                if k is None:
                    ins = dve.tensor_tensor(out, src, rstd[:, :], ALU.mult)
                else:
                    ins = dve.scalar_tensor_tensor(out=out, in0=src, scalar=k, in1=rstd[:, :], op0=ALU.mult,
                                                   op1=ALU.mult)
                ins.then_inc(tile_evicted, 1)
                dve.wait_ge(tile_evicted, at(T + 1, tper, i))

            def ffn(g, T, f_from, norm_at):
                for half, n in enumerate(FF_HALVES):
                    def body(i, first):
                        for jj in range(2):
                            f = f_from + jj
                            split_lo(g + 4 * jj + 4, 8, i)
                            dve.wait_ge(piece_done, at(g + 4 * jj + 2, 8, i))
                            if first and jj == 0:
                                norm_factor(norm_at, rstd)
                            evict_scaled(T + 2 * jj, 4, i, scr[:, jj, :])
                            split_lo(g + 4 * jj + 6, 8, i)
                            dve.wait_ge(piece_done, at(g + 4 * jj + 4, 8, i))
                            evict_scaled(T + 2 * jj + 1, 4, i, scr[:, 3, :])
                            dve.wait_ge(gated, at(f + 1, 2, i))
                            dve.tensor_tensor(scr[:, 4, :], scr[:, 5 + jj, :], scr[:, 3, :], ALU.mult).then_inc(h_f32, 1)
                            dve.wait_ge(h_hi, at(f + 1, 2, i))
                            k = jj if i is None else i * 2 + jj
                            dve.tensor_tensor(hl[:, k, :], scr[:, 4, :], hh[:, k, :].bitcast(F32), ALU.subtract)\
                               .then_inc(h_ready, 1)
                    start = 0
                    if half == 0:
                        body(None, True)
                        start = 1
                    with dve.Fori(start, n // 2) as i:
                        body(i, False)
                    T, g = T + 2 * n, g + UP_PIECES[half]
                    tiles = 4 if half == 0 else 8
                    per = tiles * n // CH
                    loops = XC // tiles
                    with dve.Fori(0, loops if g + per * loops < PIECES else loops - 1) as i:
                        down_body(g, T, tiles, n, per, i, half, 0)
                    if g + per * loops >= PIECES:
                        down_body(g + per * (loops - 1), T + tiles * (loops - 1), tiles, n, per, None, half,
                                  tiles * (loops - 1))
                    T, g, f_from = T + XC, g + DOWN_PIECES[half], f_from + n

            def down_body(g, T, tiles, n, per, i, half, d0):
                t = 0
                for p in range(per):
                    split_lo(g + p + LOOK, per, i)
                    if (p + 1) * CH >= (t + 1) * n:
                        dve.wait_ge(piece_done, at(g + p + 1, per, i))
                        out = y[:, at(d0 + t, tiles, i), :]
                        src = bank[(T + t) % 4][:, 0:TOK]
                        if half == 0:
                            ins = dve.tensor_copy(out, src)
                        else:
                            ins = dve.tensor_tensor(out, src, out, ALU.add)
                        ins.then_inc(tile_evicted, 1)
                        t += 1

            dve.wait_ge(vec_landed, 16)
            for g in range(LOOK):
                split_lo(g)
            for c in range(XC):
                x_lo("g_ffn1_pre", c, 0)
            ffn(0, 0, 0, 0)
            norm_factor(1, rpost)
            residual("g_ffn1_post", "g_mix_pre", XC, 0)
            norm_factor(2, rstd)

            split_lo(GATE_P + 4)
            dve.wait_ge(piece_done, GATE_P + 2)
            g_in, g_f, g_az, g_e, g_ln, g_lf, g_arg = (scr[0:H, k, :] for k in range(7))
            gates = bank[GATE_T % 4]
            dve.tensor_tensor(g_in, gates[0:H, 0:TOK], rstd[0:H, :], ALU.mult)
            dve.tensor_tensor(g_f, gates[32:32 + H, 0:TOK], rstd[32:32 + H, :], ALU.mult).then_inc(tile_evicted, 1)
            dve.wait_ge(tile_evicted, GATE_T + 1)
            dve.wait_ge(small_landed, 32)
            dve.wait_ge(pads_ready, 2)
            dve.tensor_scalar(g_in, g_in, gv[:, 0:1], None, ALU.add)
            link(dve.tensor_scalar(g_f, g_f, gv[:, 1:2], None, ALU.add))
            dve.scalar_tensor_tensor(out=g_az, in0=g_f, scalar=-1.0, in1=g_f, op0=ALU.mult, op1=ALU.max)\
               .then_inc(az_ready, 1)
            dve.wait_ge(e_ready, 1)
            dve.tensor_scalar(g_e, g_e, 1.0, None, ALU.add).then_inc(e1_ready, 1)
            for k in range(2):
                dve.tensor_copy(padded(igp, k), compact(g_in, k))
            dve.tensor_copy(resets(igp), gv[:, 2:2 + NB].rearrange("h (b t) -> h b t", t=1))
            dve.wait_ge(ln_ready, 1)
            link(dve.scalar_tensor_tensor(out=g_lf, in0=g_f, scalar=0.0, in1=g_ln, op0=ALU.min, op1=ALU.subtract))
            for k in range(2):
                dve.tensor_copy(padded(lfb, k), compact(g_lf, k))
                last = dve.tensor_copy(padded(lfm, k), compact(g_lf, k))
            link(last)
            dve.tensor_tensor_scan(bsum[:, :], one[:, :], lfb[:, :], 0.0, ALU.mult, ALU.add)
            link(dve.tensor_tensor_scan(mrun[:, :], lfm[:, :], igp[:, :], 0.0, ALU.add, ALU.max))
            for k in range(2):
                dve.tensor_tensor(compact(rows[:, R_BM:R_BM + TOK], k), padded(bsum, k), padded(mrun, k), ALU.subtract)
                last = dve.tensor_tensor(compact(rowc[:, :], k), padded(igp, k), padded(bsum, k), ALU.subtract)
            link(last)
            dve.tensor_scalar(g_arg[:, 0:SEQ], rowc[:, 0:SEQ], rows[:, SEQ - 1:SEQ], None, ALU.add)
            bm_dec = compact(rows[:, R_BM:R_BM + TOK], 1)
            dve.tensor_tensor(compact(g_arg, 1), compact(rowc[:, :], 1),
                              bm_dec[:, :, NT - 1:NT].broadcast_to([H, NB, NT]), ALU.add)
            m0 = gv[:, 2:2 + NB].rearrange("h (b t) -> h b t", t=1)
            dve.tensor_tensor(g_in[:, 0:NS].rearrange("h (b t) -> h b t", b=NB), bm_dec,
                              m0.broadcast_to([H, NB, NT]), ALU.add).then_inc(args_ready, 1)
            dve.tensor_copy(mout[:, 0:1], mrun[:, SEQ:SEQ + 1])
            dve.tensor_copy(mout[:, 1:1 + NB].rearrange("h (b t) -> h b t", t=1),
                            padded(mrun, 1)[:, :, NT - 1:NT]).then_inc(m_ready, 1)

            def conv_taps(j, a, b):
                acc_p = scr[:, 3, 0:SEQ]
                acc_d = scr[:, 3, SEQ:TOK].rearrange("p (b t) -> p b t", b=NB)
                for k in range(a, b):
                    w = wcur[:, j, k:k + 1]
                    if k == 0:
                        dve.tensor_scalar(acc_p, up_prompt(j, SEQ), w, bcur[:, j:j + 1], ALU.mult, ALU.add)
                        ins = dve.tensor_scalar(acc_d, up_dec(j, NT), w, bcur[:, j:j + 1], ALU.mult, ALU.add)
                    else:
                        dve.scalar_tensor_tensor(out=acc_p, in0=up_prompt(j, SEQ, k), scalar=w, in1=acc_p,
                                                 op0=ALU.mult, op1=ALU.add)
                        ins = dve.scalar_tensor_tensor(out=acc_d, in0=up_dec(j, NT, k), scalar=w, in1=acc_d,
                                                       op0=ALU.mult, op1=ALU.add)
                    link(ins)

            HEAD_LINKS = 72
            with dve.Fori(0, H) as h:
                chain.enter(h, HEAD_LINKS)
                k_, v_ = qkvo[:, 1, :, :], qkvo[:, 2, :, :]
                for q in range(HEAD_TILES):
                    split_lo(HEAD_P + 2 * q + 4, 2 * HEAD_TILES, h)
                    dve.wait_ge(piece_done, at(HEAD_P + 2 * q + 2, 2 * HEAD_TILES, h))
                    T = HEAD_T + q
                    if q == 0:
                        evict_scaled(T, HEAD_TILES, h, scr[:, 0, :])
                        dve.tensor_copy(wcur[:, :, :].rearrange("p c t -> p (c t)"),
                                        vec[:, bass.ds(h * (2 * TAPS) + V_TAP, 2 * TAPS)])
                        dve.tensor_copy(bcur[:, :], vec[:, bass.ds(h * 2 + V_BDW, 2)])
                        dve.tensor_scalar(sel[:, :], ones[0:H, :], ident[0:H, bass.ds(h, 1)], None,
                                          ALU.mult).then_inc(sel_ready, 1)
                        dve.wait_ge(sel_ready, at(1, 1, h))
                    elif q == 1:
                        evict_scaled(T, HEAD_TILES, h, scr[:, 1, :])
                    elif q == 2:
                        dve.wait_ge(u_ready, at(1, 2, h))
                        evict_scaled(T, HEAD_TILES, h, scr[:, 0, :])
                        conv_taps(0, 0, 8)
                    elif q == 3:
                        evict_scaled(T, HEAD_TILES, h, scr[:, 1, :])
                        conv_taps(0, 8, 16)
                    elif q in (4, 5):
                        evict_scaled(T, HEAD_TILES, h, k_[:, q - 4, :], DH ** -0.5)
                        conv_taps(0, 16 + 8 * (q - 4), min(24 + 8 * (q - 4), TAPS))
                        if q == 4:
                            dve.wait_ge(rowsT_done, at(3, 3, h))
                            dve.tensor_copy(colc[:, :].rearrange("p (k o) -> p k o", o=1),
                                            bank[4][:, 0:4 * H].rearrange("p (k h) -> p k h", h=H)[:, :, bass.ds(h, 1)])
                            dve.tensor_copy(cols[:, :].rearrange("p (k o) -> p k o", o=1),
                                            bank[4][0:NS, 4 * H:6 * H].rearrange("p (k h) -> p k h", h=H)
                                            [:, :, bass.ds(h, 1)]).then_inc(col_ready, 1)
                            dve.wait_ge(col_ready, at(1, 1, h))
                            dve.tensor_scalar(gkm[:, :], mask[:, :], cols[:, 1:2], None, ALU.mult)
                        else:
                            dve.tensor_copy(yc[:, h * 2, :], scr[:, 3, :]).then_inc(conv_done, 1)
                            dve.wait_ge(conv_done, at(1, 2, h))
                    elif q in (6, 7):
                        evict_scaled(T, HEAD_TILES, h, v_[:, q - 6, :])
                        dve.wait_ge(u_ready, at(2, 2, h))
                        conv_taps(1, 8 * (q - 6), 8 * (q - 5))
                    elif q in (8, 9):
                        evict_scaled(T, HEAD_TILES, h, qkvo[:, 0, q - 8, :])
                        if q == 8:
                            dve.wait_ge(tr_done, at(1, 3, h))
                            dve.tensor_copy(vs[:, :], bank[7][0:NS, 0:DH])
                            dve.tensor_copy(ks[:, :], bank[7][0:NS, DH:2 * DH]).then_inc(tr_evicted, 1)
                            dve.wait_ge(tr_done, at(2, 3, h))
                            dve.tensor_copy(vtok[:, :, :].rearrange("p t e -> p (t e)"), bank[5][:, :])\
                               .then_inc(tr_evicted, 1)
                            dve.wait_ge(tr_done, at(3, 3, h))
                            dve.tensor_scalar(ktg[:, 0, :], bank[6][:, 0:DH], colc[:, 2:3], None, ALU.mult)
                            dve.tensor_scalar(ktg[:, 1, :], bank[6][:, DH:2 * DH], colc[:, 3:4], None, ALU.mult)\
                               .then_inc(tr_evicted, 1)
                            dve.wait_ge(tr_evicted, at(3, 3, h))
                            for b in range(NB):
                                last = dve.tensor_scalar(ksm[:, b, :], ks[:, :], gkm[:, b:b + 1], None, ALU.mult)
                            last.then_inc(ksm_ready, 1)
                            conv_taps(1, 16, 20)
                        else:
                            dve.wait_ge(bc_ready, at(2, 2, h))
                            wi = bc[:, R_WI:ROWS].rearrange("p (o t) -> p o t", o=1).broadcast_to([P, DC, NS])
                            link(dve.tensor_tensor(qw[:, :, :], qkvo[:, 0, :, SEQ:TOK], wi, ALU.mult))
                            for c in range(DC):
                                last = dve.tensor_tensor(
                                    qwn[:, c, :].rearrange("p (b t) -> p b t", b=NB),
                                    qw[:, c, :].rearrange("p (b t) -> p b t", b=NB),
                                    n0[:, bass.ds(h, 1), c, :].rearrange("p o b -> p b o").broadcast_to([P, NB, NT]),
                                    ALU.mult)
                            last.then_inc(qw_ready, 1)
                            conv_taps(1, 20, 26)
                    elif q == 10:
                        evict_scaled(T, HEAD_TILES, h, scr[:, 0, :])
                        dve.wait_ge(qc_done, at(1, 1, h))
                        dve.tensor_copy(qcs[:, :, :].rearrange("p c t -> p (c t)"), bank[7][:, 0:DC * NS])\
                           .then_inc(qc_evicted, 1)
                        for b in range(NB + 1):
                            dve.wait_ge(cu_done, at(b + 1, NB + 1, h))
                            src = bank[5 + b % 2][:, :]
                            if b < NB:
                                Cb = C[:, b, :, :].rearrange("p c e -> p (c e)")
                                g_st = bc[:, R_WI + b * NT + NT - 1:R_WI + (b + 1) * NT]
                                dve.scalar_tensor_tensor(out=Cb, in0=Cb, scalar=g_st, in1=src, op0=ALU.mult,
                                                         op1=ALU.add).then_inc(cu_evicted, 1)
                            else:
                                dve.wait_ge(stored, at(48, 48, h))
                                dve.tensor_copy(cpr[:, :, :].rearrange("p c e -> p (c e)"), src)\
                                   .then_inc(cu_evicted, 1)
                        dve.wait_ge(sc_done, at(1, 1, h))
                        dve.wait_ge(w_ready, at(1, 1, h))
                        n = SEQ + P
                        dve.tensor_tensor(st[:, 0:n], bank[4][:, 0:n], wt[:, 0:n], ALU.mult)
                        dve.tensor_tensor(st[0:NS, n:n + NS], bank[4][0:NS, n:n + NS], wt[0:NS, n:n + NS],
                                          ALU.mult).then_inc(st_ready, 1)
                        conv_taps(1, 26, TAPS)
                        dve.tensor_copy(yc[:, h * 2 + 1, :], scr[:, 3, :]).then_inc(conv_done, 1)
                        dve.wait_ge(conv_done, at(2, 2, h))
                    else:
                        evict_scaled(T, HEAD_TILES, h, scr[:, 1, :])
                        dve.wait_ge(kg_ready, at(1, 1, h))
                        dve.tensor_reduce(nnp[:, bass.ds(h, 1), :].rearrange("p o c -> p (o c)"),
                                          scr[:, 5:7, 0:SEQ], AX_X, ALU.add)
                        link(dve.tensor_reduce(nred[:, :, :].rearrange("p c b -> p (c b)"),
                                               scr[:, 5:7, SEQ:TOK].rearrange("p c (b t) -> p c b t", b=NB), AX_X,
                                               ALU.add))
                        g_st = bc[:, R_WI:ROWS].rearrange("p (b t) -> p b t", b=NB)[:, :, NT - 1:NT]
                        for c in range(DC):
                            last = dve.tensor_tensor(scr[:, 2, c * NB:(c + 1) * NB],
                                                     n0[:, bass.ds(h, 1), c, :].rearrange("p o b -> p (o b)"),
                                                     g_st.rearrange("p b t -> p (b t)"), ALU.mult)
                        link(last)
                        dve.tensor_tensor(nns[:, bass.ds(h, 1), :, :].rearrange("p o c b -> p (o c b)"),
                                          scr[:, 2, 0:DC * NB], nred[:, :, :].rearrange("p c b -> p (c b)"), ALU.add)\
                           .then_inc(nn_ready, 1)
                        dve.wait_ge(nn_ready, at(1, 1, h))
                        dve.wait_ge(num_done, at(1, 3, h))
                        link(dve.tensor_copy(scr[:, 2, :], bank[7][:, 0:TOK]))
                        link(dve.scalar_tensor_tensor(out=scr[:, 2, :], in0=scr[:, 2, :], scalar=-1.0,
                                                      in1=scr[:, 2, :], op0=ALU.mult, op1=ALU.max))
                        link(dve.tensor_tensor(scr[:, 2, :], scr[:, 2, :], bc[:, R_EM:R_EM + TOK], ALU.max))
                        dve.reciprocal(scr[:, 2, :], scr[:, 2, :]).then_inc(hm_num, 1)
                        for e in range(DC):
                            dve.wait_ge(num_done, at(e + 2, 3, h))
                            dve.wait_ge(hm_num, at(e + 1, 3, h))
                            link(dve.tensor_copy(scr[:, 4 + e, :], bank[5 + e][:, 0:TOK]))
                            link(dve.tensor_tensor(scr[:, 4 + e, SEQ:TOK], scr[:, 4 + e, SEQ:TOK], qcs[:, e, :],
                                                   ALU.add))
                            dve.tensor_tensor(scr[:, 4 + e, :], scr[:, 4 + e, :], scr[:, 2, :], ALU.mult)\
                               .then_inc(hm_num, 1)
                        for e in range(DC):
                            dve.wait_ge(hm_hi, at(e + 1, 2, h))
                            dve.tensor_tensor(ml[:, h * DC + e, :], scr[:, 4 + e, :],
                                              mh[:, h * DC + e, :].bitcast(F32), ALU.subtract).then_inc(mix_ready, 1)
            chain.leave(H)

            dve.wait_ge(ln_sum, 1)
            link(dve.tensor_scalar(scr[:, 0, :], bank[4][:, 0:TOK], 1.0 / D_CONV, None, ALU.mult))
            for c in range(CC):
                dve.tensor_tensor(yc[:, c, :], yc[:, c, :], scr[:, 0, :], ALU.subtract).then_inc(ln_cent, 1)
            dve.wait_ge(ln_sqsum, 1)
            dve.tensor_scalar(scr[:, 5, :], bank[5][:, 0:TOK], 1.0 / D_CONV, EPS, ALU.mult, ALU.add)\
               .then_inc(ln_var, 1)
            dve.wait_ge(ln_sd, 1)
            link(dve.reciprocal(scr[:, 1, :], scr[:, 6, :]))
            for c in range(CC):
                dve.tensor_tensor(yc[:, c, :], yc[:, c, :], scr[:, 1, :], ALU.mult).then_inc(ln_yn, 1)
                dve.wait_ge(ln_yn, c + 1)
                dve.tensor_scalar(sq8[:, c, :], yc[:, c, :], vec[:, V_GLN + c:V_GLN + c + 1],
                                  vec[:, V_BLN + c:V_BLN + c + 1], ALU.mult, ALU.add).then_inc(ln_z, 1)
            split_lo(OUT_P + 4)
            for c in range(CC):
                dve.wait_ge(ln_hi, c + 1)
                dve.tensor_tensor(xh[:, CC + c, :], yc[:, c, :], xh[:, c, :].bitcast(F32), ALU.subtract)\
                   .then_inc(conv_ready, 1)
            split_lo(OUT_P + 6)

            def out_body(i):
                for p in range(8):
                    if i is not None or p >= 4:
                        split_lo(OUT_P + p + LOOK, 8, i)
                    if p >= 4:
                        t = p - 4
                        dve.wait_ge(piece_done, at(OUT_P + p + 1, 8, i))
                        dve.tensor_copy(y[:, at(t, 4, i), :], bank[(OUT_T + t) % 4][:, 0:TOK]).then_inc(tile_evicted, 1)

            dve.wait_ge(stored, 32 + 48 * H)
            out_body(None)
            with dve.Fori(1, XC // 4) as i:
                out_body(i)
            norm_factor(3, rpost)
            residual("g_mix_post", "g_ffn2_pre", 2 * XC, XC)
            dve.wait_ge(small_stored, 32)
            ffn(FFN2_P, FFN2_T, sum(FF_HALVES), 4)
            norm_factor(5, rpost)
            residual("g_ffn2_post", None, 0, 2 * XC)

        @block.gpsimd
        def _(pool):
            def split_lo(g, per=0, i=None):
                if g % 2 == 0 or g >= PIECES:
                    return
                pool.wait_ge(hi_ready, at(g + 1, per, i))
                pool.tensor_tensor(wlo[:, g % SLOTS, :], raw[:, g % SLOTS, :], whi[:, g % SLOTS, :].bitcast(F32),
                                   ALU.subtract).then_inc(lo_ready[1], 1)

            def clear_ssq(k):
                if k:
                    pool.wait_ge(norm_sum, k)
                pool.memset(ssq[:, :], 0.0).then_inc(ssq_clear, 1)
                pool.wait_ge(ssq_clear, k + 1)

            def add_sq(n, per=0, i=None):
                pool.wait_ge(sq_ready, at(n + 1, per, i))
                pool.tensor_tensor(ssq[:, :], ssq[:, :], sq[:, n % 2, :], ALU.add).then_inc(ssq_added, 1)
                pool.wait_ge(ssq_added, at(n + 1, per, i))

            def ffn(g, T, f_from, sq_from, norm_at):
                for half, n in enumerate(FF_HALVES):
                    with pool.Fori(0, n // 2) as i:
                        for jj in range(2):
                            f = f_from + jj
                            split_lo(g + 4 * jj + 3, 8, i)
                            pool.wait_ge(sig_ready, at(f + 1, 2, i))
                            pool.tensor_tensor(scr[:, 5 + jj, :], scr[:, jj, :], scr[:, 2, :], ALU.mult).then_inc(gated, 1)
                            split_lo(g + 4 * jj + 5, 8, i)
                    T, g = T + 2 * n, g + UP_PIECES[half]
                    tiles = 4 if half == 0 else 8
                    per = tiles * n // CH
                    loops = XC // tiles
                    if half == 0:
                        clear_ssq(norm_at + 1)
                    with pool.Fori(0, loops if g + per * loops < PIECES else loops - 1) as i:
                        down_body(g, tiles, n, per, i, half, sq_from)
                    if g + per * loops >= PIECES:
                        down_body(g + per * (loops - 1), tiles, n, per, None, half, sq_from + tiles * (loops - 1))
                    T, g, f_from = T + XC, g + DOWN_PIECES[half], f_from + n

            def down_body(g, tiles, n, per, i, half, sq_from):
                t = 0
                for p in range(per):
                    split_lo(g + p + LOOK, per, i)
                    if (p + 1) * CH >= (t + 1) * n:
                        if half == 1:
                            add_sq(sq_from + t, tiles, i)
                        t += 1

            pool.memset(ident[:, :], 0.0).then_inc(pool_chain, 1)
            pool.memset(ones[:, :], 1.0)
            pool.wait_ge(pool_chain, 1)
            pool.affine_select(out=ident[:, :], in_=ident[:, :], compare_op=ALU.not_equal, fill=1.0, base=0,
                               pattern=[[-1, P]], channel_multiplier=1).then_inc(consts_ready, 1)
            clear_ssq(0)
            for g in range(LOOK):
                split_lo(g)
            for c in range(XC):
                add_sq(c)
            ffn(0, 0, 0, XC, 0)
            clear_ssq(2)
            pool.dma_start(gv[:, :], gate_vec).then_inc(small_landed, 16)
            pool.dma_start(n0[:, :, :, :], n_in).then_inc(small_landed, 16)
            pool.memset(lfb[:, :], 0.0)
            pool.memset(lfm[:, :], -3.0e38)
            pool.memset(igp[:, :], 0.0)
            pool.memset(mask[:, :], 1.0)
            pool.memset(one[:, :], 1.0).then_inc(pads_ready, 1)
            pool.wait_ge(pads_ready, 1)
            pool.memset(resets(one), 0.0)
            pool.memset(one[:, 0:1], 0.0)
            for j in range(2):
                pool.memset(up_prompt(j, HIST), 0.0)
            pool.affine_select(out=mask[:, :], in_=mask[:, :], compare_op=ALU.is_ge, fill=0.0, base=0,
                               pattern=[[-NT, NB]], channel_multiplier=1).then_inc(pool_chain, 1)
            pool.wait_ge(pool_chain, 2)
            pool.affine_select(out=mask[:, :], in_=mask[:, :], compare_op=ALU.is_ge, fill=0.0, base=NT - 1,
                               pattern=[[NT, NB]], channel_multiplier=-1).then_inc(pads_ready, 1)
            for c in range(XC):
                add_sq(2 * XC + c)
            pool.memset(ysum, 0.0)
            split_lo(GATE_P + 3)
            clear_ssq(3)

            with pool.Fori(0, H) as h:
                for q in range(HEAD_TILES):
                    split_lo(HEAD_P + 2 * q + 3, 2 * HEAD_TILES, h)
                    if q in (1, 3):
                        j = q // 2
                        pool.wait_ge(sigb_ready, at(j + 1, 2, h))
                        pool.wait_ge(hist_ready, at(2, 2, h))
                        pool.tensor_tensor(up_prompt(j, SEQ, HIST), scr[:, 0, 0:SEQ], scr[:, 2, 0:SEQ], ALU.mult)
                        pool.tensor_tensor(up_dec(j, NT, HIST),
                                           scr[:, 0, SEQ:TOK].rearrange("p (b t) -> p b t", b=NB),
                                           scr[:, 2, SEQ:TOK].rearrange("p (b t) -> p b t", b=NB), ALU.mult)\
                            .then_inc(u_ready, 1)
                    if q == 6:
                        pool.wait_ge(w_exp, at(1, 1, h))
                        pool.wait_ge(tile_evicted, at(HEAD_T + 6, HEAD_TILES, h))
                        pool.wait_ge(bc_ready, at(2, 2, h))
                        pool.tensor_tensor(scr[:, 5, :], qkvo[:, 1, 0, :], bc[:, R_GK:R_GK + TOK], ALU.mult)
                        diag = wt[:, 0:2 * SEQ - P].rearrange("p (k l) -> p k l", l=P)[:, 0:3:2, :]
                        pool.affine_select(out=diag, in_=diag, compare_op=ALU.is_ge, fill=0.0, base=0,
                                           pattern=[[0, 2], [1, P]], channel_multiplier=-1)
                        dec = wt[0:NS, SEQ + P:SEQ + P + NS].rearrange("p (b t) -> p b t", b=NB)
                        pool.affine_select(out=dec, in_=dec, compare_op=ALU.is_ge, fill=0.0, base=0,
                                           pattern=[[NT, NB], [1, NT]], channel_multiplier=-1).then_inc(pool_chain, 1)
                        pool.wait_ge(pool_chain, at(3, 1, h))
                        pool.tensor_tensor(scr[:, 6, :], qkvo[:, 1, 1, :], bc[:, R_GK:R_GK + TOK], ALU.mult)\
                            .then_inc(kg_ready, 1)
                        pool.affine_select(out=dec, in_=dec, compare_op=ALU.is_ge, fill=0.0, base=0,
                                           pattern=[[-NT, NB], [0, NT]], channel_multiplier=1).then_inc(w_ready, 1)
                    if q in (6, 10):
                        j = 0 if q == 6 else 1
                        pool.wait_ge(conv_done, at(j + 1, 2, h))
                        pool.tensor_tensor(ysum, ysum, yc[:, h * 2 + j, :], ALU.add).then_inc(ysum_added, 1)
                        pool.wait_ge(ysum_added, at(j + 1, 2, h))
                    if q == 11:
                        for e in range(DC):
                            pool.wait_ge(hm_num, at(e + 2, 3, h))
                            pool.wait_ge(osig_ready, at(e + 1, 2, h))
                            pool.tensor_tensor(scr[:, 4 + e, :], scr[:, 4 + e, :], qkvo[:, 3, e, :], ALU.mult)\
                                .then_inc(hm_ready, 1)

            pool.wait_ge(nn_ready, H)
            pool.dma_start(ns_out, nns[:, :, :, :]).then_inc(small_stored, 16)
            pool.dma_start(np_out, nnp[:, :, :]).then_inc(small_stored, 16)
            split_lo(OUT_P + 3)
            for c in range(CC):
                pool.wait_ge(ln_sig, c + 1)
                pool.wait_ge(ln_z, c + 1)
                pool.tensor_tensor(yc[:, c, :], sq8[:, c, :], sg8[:, c, :], ALU.mult).then_inc(ln_silu, 1)
            split_lo(OUT_P + 5)

            def out_body(i):
                for p in range(8):
                    if i is not None or p >= 4:
                        split_lo(OUT_P + p + LOOK, 8, i)
                    if p >= 4:
                        add_sq(3 * XC + p - 4, 4, i)

            out_body(None)
            with pool.Fori(1, XC // 4) as i:
                out_body(i)
            clear_ssq(4)
            for c in range(XC):
                add_sq(4 * XC + c)
            ffn(FFN2_P, FFN2_T, sum(FF_HALVES), 5 * XC, 4)


def _pieces(w, order):
    chunks = w.reshape(w.shape[0] // P, P, w.shape[1] // P, P)
    flat = np.array(order).reshape(-1, CH, 2)
    out = chunks[flat[:, :, 1], :, flat[:, :, 0], :]
    return np.ascontiguousarray(out.transpose(0, 2, 1, 3)).reshape(len(flat), P, PIECE)


def _ffn_pieces(gate, up, down):
    parts, f0 = [], 0
    gu = np.concatenate([gate, up], axis=1)
    up_tile = D_FF // P
    for n in FF_HALVES:
        parts.append(_pieces(gu, [(t, k) for f in range(f0, f0 + n) for t in (f, up_tile + f) for k in range(XC)]))
        parts.append(_pieces(down, [(t, f0 + k) for t in range(XC) for k in range(n)]))
        f0 += n
    return parts


def _feature_major(a):
    return a.T.reshape(-1, P, a.shape[0]).transpose(1, 0, 2)


def kernel(**inputs):
    import concourse.bacc as bacc
    from concourse.bass_utils import run_bass_kernel_spmd

    a = {k: np.asarray(v) for k, v in inputs.items()}
    w_in = a["w_in"][0]
    gates = np.zeros((D_MODEL, P), np.float32)
    gates[:, 0:H] = w_in[:, 6 * D_MLSTM:6 * D_MLSTM + H]
    gates[:, 32:32 + H] = w_in[:, 6 * D_MLSTM + H:]
    per = D_MLSTM // P
    q0, k0, v0, o0, a0, b0 = (n * per for n in range(6))
    tiles = []
    for h in range(H):
        for c in range(2):
            tiles += [a0 + 2 * h + c, b0 + 2 * h + c]
        for base in (k0, v0, q0, o0):
            tiles += [base + DC * h, base + DC * h + 1]
    out_order = [(4 * g + q, half * CH + k) for g in range(XC // 4) for half in range(2) for q in range(4)
                 for k in range(CH)]
    stream = np.concatenate(
        _ffn_pieces(a["w_ffn1_gate"][0], a["w_ffn1_up"][0], a["w_ffn1_down"][0])
        + [_pieces(gates, [(0, k) for k in range(XC)]),
           _pieces(w_in[:, :6 * D_MLSTM], [(t, k) for t in tiles for k in range(XC)]),
           _pieces(a["w_out"][0], out_order)]
        + _ffn_pieces(a["w_ffn2_gate"][0], a["w_ffn2_up"][0], a["w_ffn2_down"][0]))
    assert len(stream) == PIECES
    col = lambda v: v.reshape(-1, P).T
    vecs = np.concatenate(
        [col(a[g][0]) for g in GAINS]
        + [a["w_dw"][0].T.reshape(CC, P, TAPS).transpose(1, 0, 2).reshape(P, CC * TAPS)]
        + [col(a[g][0]) for g in ("b_dw", "g_conv_ln", "b_conv_ln")], axis=1)
    x_in = np.concatenate([_feature_major(a["x_prompt"][0]), _feature_major(a["x_sample"].reshape(NS, D_MODEL))], axis=2)
    gate_vec = np.concatenate([a["b_igate"].T, a["b_fgate"].T, a["state_mlstm_m"][0].T], axis=1)
    c_in = a["state_mlstm_C"][0].reshape(NB, H, DC, P, DH).transpose(1, 3, 0, 2, 4)
    n_in = a["state_mlstm_n"][0].reshape(NB, H, DC, P).transpose(3, 1, 2, 0)
    conv_in = a["state_conv"][0].transpose(2, 0, 1).reshape(H, 2, P, NB * HIST).transpose(0, 2, 1, 3)
    arrays = {"stream": stream, "x_in": x_in, "vecs": vecs, "gate_vec": gate_vec, "c_in": c_in, "n_in": n_in,
              "conv_in": conv_in}
    arrays = {k: np.ascontiguousarray(v) for k, v in arrays.items()}
    outs = {"y_out": (P, XC, TOK), "cp_out": (H, P, DC, DH), "np_out": (P, H, DC), "cs_out": (H, P, NB, DC, DH),
            "ns_out": (P, H, DC, NB), "m_out": (H, 1 + NB), "conv_out": (H, P, 2, NEW_C)}

    nc = bacc.Bacc("TRN2", target_bir_lowering=False, num_devices=1)
    args = {k: nc.dram_tensor(k, v.shape, F32, kind="ExternalInput").ap() for k, v in arrays.items()}
    args |= {k: nc.dram_tensor(k, s, F32, kind="ExternalOutput").ap() for k, s in outs.items()}
    hybrid_layer_kernel(nc, **args)
    r = run_bass_kernel_spmd(nc, [arrays], core_ids=[0]).results[0]

    y = r["y_out"].transpose(2, 1, 0).reshape(TOK, D_MODEL)
    conv = r["conv_out"].transpose(3, 0, 2, 1).reshape(NEW_C, D_CONV)
    return (y[:SEQ].reshape(1, SEQ, D_MODEL), y[SEQ:].reshape(NB, NT, D_MODEL),
            r["cp_out"].transpose(0, 2, 1, 3).reshape(1, 1, H, DH, DH),
            r["np_out"].transpose(1, 2, 0).reshape(1, 1, H, DH),
            r["m_out"][:, 0].reshape(1, 1, H),
            conv[:HIST].reshape(1, 1, HIST, D_CONV),
            r["cs_out"].transpose(2, 0, 3, 1, 4).reshape(1, NB, H, DH, DH),
            r["ns_out"].transpose(3, 1, 2, 0).reshape(1, NB, H, DH),
            r["m_out"][:, 1:].T.reshape(1, NB, H),
            conv[HIST:].reshape(NB, HIST, D_CONV)[None])
```

```python
from contextlib import ExitStack

import concourse.bass as bass
import concourse.mybir as mybir
import numpy as np

F32 = mybir.dt.float32
F32R = mybir.dt.float32r
ALU = mybir.AluOpType
ACT = mybir.ActivationFunctionType
AX_X = mybir.AxisListType.X

P = 128
D_MODEL = 2048
D_FF = 5632
SEQ = 256
NB, NT = 8, 4
NS = NB * NT
TOK = SEQ + NS
H, DH = 4, 256
DC = DH // P
D_MLSTM = H * DH
D_CONV = D_MODEL - D_MLSTM
TAPS = 31
HIST = TAPS - 1
EPS = 1e-6
XC = D_MODEL // P
CC = D_CONV // P
CH = 8
SLOTS = 4
PIECE = CH * P
FF_HALVES = (24, 20)
HEAD_TILES = 12
LOOK = 3
SQ_BUFS = 2
START_SPLITS = {0: 0, 1: 1, 2: 4, 3: 5, 4: 13}
NEXT_SPLITS = {4: 11}

UP_PIECES = [2 * n * XC // CH for n in FF_HALVES]
DOWN_PIECES = [XC * n // CH for n in FF_HALVES]
FFN_PIECES = sum(UP_PIECES) + sum(DOWN_PIECES)
FFN_TILES = sum(2 * n + XC for n in FF_HALVES)
GATE_P, GATE_T = FFN_PIECES, FFN_TILES
HEAD_P, HEAD_T = GATE_P + XC // CH, GATE_T + 1
OUT_P, OUT_T = HEAD_P + H * HEAD_TILES * XC // CH, HEAD_T + H * HEAD_TILES
FFN2_P, FFN2_T = OUT_P + XC * XC // CH, OUT_T + XC
PIECES = FFN2_P + FFN_PIECES

GAINS = ("g_ffn1_pre", "g_ffn1_post", "g_mix_pre", "g_mix_post", "g_ffn2_pre", "g_ffn2_post")
V_TAP = len(GAINS) * XC
V_BDW = V_TAP + CC * TAPS
V_GLN = V_BDW + CC
V_BLN = V_GLN + CC
VEC = V_BLN + CC

R_BM, R_EM, R_GK, R_WI, ROWS = 0, TOK, 2 * TOK, 3 * TOK, 3 * TOK + NS
PADT = 1 + SEQ + NB * (1 + NT)
UP_W = HIST + SEQ + NB * (HIST + NT)
NEW_C = HIST * (1 + NB)


def at(base, per, i):
    return base if i is None else i * per + base


class Chain:

    def __init__(self, eng, sem):
        self.eng, self.sem, self.base, self.k, self.i, self.per = eng, sem, 0, 0, None, 0

    def link(self, ins):
        ins.then_inc(self.sem, 1)
        self.k += 1
        self.eng.wait_ge(self.sem, at(self.base + self.k, self.per, self.i))

    def enter(self, i, per):
        self.base, self.k, self.i, self.per = self.base + self.k, 0, i, per

    def leave(self, times):
        assert self.k == self.per, (self.k, self.per)
        self.base, self.k, self.i, self.per = self.base + self.per * times, 0, None, 0


def hybrid_layer_kernel(nc, stream, x_in, vecs, gate_vec, c_in, n_in, conv_in,
                        y_out, cp_out, np_out, cs_out, ns_out, m_out, conv_out):
    with ExitStack() as ctx:
        def sb(name, shape, dt=F32):
            return ctx.enter_context(nc.sbuf_tensor(name, shape, dt))

        def sem(name):
            return ctx.enter_context(nc.semaphore(name))

        x = sb("x_res", [P, XC, TOK])
        xh = sb("xh", [P, XC, TOK], F32R)
        raw = sb("raw", [P, SLOTS, PIECE])
        whi = sb("whi", [P, SLOTS, PIECE], F32R)
        wlo = sb("wlo", [P, SLOTS, PIECE], F32R)
        vec = sb("vec", [P, VEC])
        ones = sb("ones", [P, P])
        ident = sb("ident", [P, P])
        rstd = sb("rstd", [P, TOK])
        rpost = sb("rpost", [P, TOK])
        ssq = sb("ssq", [P, TOK])
        warm = sb("warm", [P, 8])
        sq = sb("sq", [P, 2, TOK])
        scr = sb("scr", [P, 7, TOK])

        arena = [-(-nc.sbuf_base // 32) * 32]
        pad_bytes = -(-4 * PADT // 32) * 32

        def place(name, shape, dt=F32, where=None):
            t = nc.alloc_sbuf_tensor_at(name, shape, dt, offset=where if where is not None else arena[0])
            if where is None:
                arena[0] += -(-4 * int(np.prod(shape[1:])) // 32) * 32
            return t

        xl = place("xl", [P, XC, TOK], F32R)
        mix_at = arena[0]
        hh = place("hh", [P, FF_HALVES[0], TOK], F32R)
        hl = place("hl", [P, FF_HALVES[0], TOK], F32R)
        y_at = arena[0]
        y = place("y", [P, XC, TOK])
        y_end = arena[0]
        assert arena[0] <= nc.sbuf_usable_end, arena
        arena[0] = mix_at
        mh = place("mh", [P, D_MLSTM // P, TOK], F32R)
        ml = place("ml", [P, D_MLSTM // P, TOK], F32R)
        qkvo = place("qkvo", [P, 4, DC, TOK])
        yc = place("yc", [P, CC, TOK])
        c_at = arena[0]
        C = place("C", [P, NB, DC, DH])
        lfb = place("lfb", [H, PADT], F32, c_at)
        lfm = place("lfm", [H, PADT], F32, c_at + pad_bytes)
        igp = place("igp", [H, PADT], F32, c_at + 2 * pad_bytes)
        one = place("one", [H, PADT], F32, c_at + 3 * pad_bytes)
        bsum = place("bsum", [H, PADT], F32, c_at + 4 * pad_bytes)
        mrun = place("mrun", [H, PADT], F32, c_at + 5 * pad_bytes)
        cpr = place("cpr", [P, DC, DH])
        rows = place("rows", [H, ROWS])
        rowc = place("rowc", [H, TOK])
        bc = place("bc", [P, ROWS])
        vtok = place("vtok", [P, 2, DH])
        ktg = place("ktg", [P, 2, DH])
        vs = place("vs", [NS, DH])
        ksm = place("ksm", [NS, NB, DH])
        wt = place("wt", [P, SEQ + P + NS])
        st = place("st", [P, SEQ + P + NS])
        upad = place("upad", [P, 2, UP_W])
        hist = place("hist", [P, 2, NB * HIST])
        newc = place("newc", [P, 2, NEW_C])
        wcur = place("wcur", [P, 2, TAPS])
        bcur = place("bcur", [P, 2])
        ysum = sq[:, 0, :]
        sel = place("sel", [H, P])
        colc = place("colc", [P, 4])
        cols = place("cols", [NS, 2])
        gkm = place("gkm", [NS, NB])
        mask = place("mask", [NS, NB])
        gv = place("gv", [H, 2 + NB])
        n0 = place("n0", [P, H, DC, NB])
        nns = place("nns", [P, H, DC, NB])
        nnp = place("nnp", [P, H, DC])
        nred = place("nred", [P, DC, NB])
        qwn = place("qwn", [P, DC, NS])
        qct = place("qct", [NS, DH])
        mout = place("mout", [H, 1 + NB])
        assert arena[0] <= nc.sbuf_usable_end, (arena, nc.sbuf_usable_end)
        sq8 = qkvo[:, :, :, :].rearrange("p a b t -> p (a b) t")
        sg8 = C[:, :, :, :].rearrange("p b c e -> p (b c e)")[:, 0:CC * TOK].rearrange("p (c t) -> p c t", c=CC)

        bank = [ctx.enter_context(nc.psum_tensor(f"bank{i}", [P, 512], F32)) for i in range(8)]

        landed = [sem(f"piece_landed{s}") for s in range(SLOTS)]
        x_landed = [sem(f"x_landed{c}") for c in range(4)]
        vec_landed, small_landed = sem("vec_landed"), sem("small_landed")
        hi_ready = sem("hi_ready")
        lo_ready = [sem("lo_ready_even"), sem("lo_ready_odd")]
        piece_done = sem("piece_done")
        tile_evicted = sem("tile_evicted")
        consts_ready = sem("consts_ready")
        x_hi, x_ready, x_new = sem("x_hi"), sem("x_ready"), sem("x_new")
        sq_ready, ssq_added, ssq_clear = sem("sq_ready"), sem("ssq_added"), sem("ssq_clear")
        xsq_ready, xsq_sum, t_ready, rpost_ready = sem("xsq_ready"), sem("xsq_sum"), sem("t_ready"), sem("rpost_ready")
        norm_sum, norm_var, norm_sd = sem("norm_sum"), sem("norm_var"), sem("norm_sd")
        sig_ready, gated, h_f32, h_hi, h_ready = (sem("sig_ready"), sem("gated"), sem("h_f32"),
                                                  sem("h_hi"), sem("h_ready"))
        dve_chain, pool_chain = sem("dve_chain"), sem("pool_chain")
        pads_ready, az_ready, e_ready, e1_ready, ln_ready = (sem("pads_ready"), sem("az_ready"), sem("e_ready"),
                                                             sem("e1_ready"), sem("ln_ready"))
        args_ready, rows_ready, m_ready = sem("args_ready"), sem("rows_ready"), sem("m_ready")
        sel_ready, rowsT_done, bc_ready, col_ready = (sem("sel_ready"), sem("rowsT_done"), sem("bc_ready"),
                                                      sem("col_ready"))
        hist_landed, hist_ready, sigb_ready, u_ready = (sem("hist_landed"), sem("hist_ready"),
                                                        sem("sigb_ready"), sem("u_ready"))
        newc_ready, conv_done, ysum_added = sem("newc_ready"), sem("conv_done"), sem("ysum_added")
        w_exp, w_ready = sem("w_exp"), sem("w_ready")
        tr_done, tr_evicted, gkm_ready, qw_ready, den_ready = (
            sem("tr_done"), sem("tr_evicted"), sem("gkm_ready"), sem("qw_ready"), sem("den_ready"))
        qc_done, qc_evicted, cu_done, cu_evicted = (sem("qc_done"), sem("qc_evicted"), sem("cu_done"),
                                                    sem("cu_evicted"))
        sc_done, st_ready, num_done, rden_ready, ro_ready = (sem("sc_done"), sem("st_ready"), sem("num_done"),
                                                             sem("rden_ready"), sem("ro_ready"))
        osig_ready, hm_ready, hm_hi, mix_ready, kg_ready = (
            sem("osig_ready"), sem("hm_ready"), sem("hm_hi"), sem("mix_ready"), sem("kg_ready"))
        c_landed, stored, out_stored, small_stored = (sem("c_landed"), sem("c_stored"), sem("out_stored"),
                                                      sem("small_stored"))
        ln_sum, ln_cent, ln_sq, ln_sqsum, ln_var, ln_sd = (
            sem("ln_sum"), sem("ln_cent"), sem("ln_sq"), sem("ln_sqsum"), sem("ln_var"), sem("ln_sd"))
        ln_yn, ln_z, ln_sig, ln_silu, ln_hi, conv_ready = (
            sem("ln_yn"), sem("ln_z"), sem("ln_sig"), sem("ln_silu"), sem("ln_hi"), sem("conv_ready"))
        nn_ready = sem("nn_ready")

        block = ctx.enter_context(nc.Block())

        def gain(name, c):
            k = GAINS.index(name) * XC + c
            return vec[:, k:k + 1]

        def padded(row, k):
            if k == 0:
                return row[:, 1:1 + SEQ]
            return row[:, 1 + SEQ:PADT].rearrange("h (b t) -> h b t", b=NB)[:, :, 1:1 + NT]

        def resets(row):
            return row[:, 1 + SEQ:PADT].rearrange("h (b t) -> h b t", b=NB)[:, :, 0:1]

        def compact(row, k):
            if k == 0:
                return row[:, 0:SEQ]
            return row[:, SEQ:TOK].rearrange("h (b t) -> h b t", b=NB)

        assert NB * (NS + NT) <= TOK and DC == 2
        qm = (sq[:, 1, 0:NB * (NS + NT)], rpost[:, 0:NB * (NS + NT)])
        qw = [q.rearrange("p (b w) -> p b w", b=NB)[:, :, 0:NT] for q in qm]

        def up_prompt(j, n, off=0):
            return upad[:, j, off:off + n]

        def up_dec(j, n, off=0):
            return upad[:, j, HIST + SEQ:UP_W].rearrange("p (b w) -> p b w", b=NB)[:, :, off:off + n]

        @block.sync
        def _(sp):
            sp.dma_start(vec[:, :], vecs).then_inc(vec_landed, 16)
            for what, n in (("w", 0), ("x", 0), ("w", 1), ("x", 1), ("w", 2), ("w", 3), ("x", 2), ("x", 3)):
                if what == "w":
                    sp.dma_start(raw[:, n, :], stream[n]).then_inc(landed[n], 16)
                else:
                    sp.dma_start(x[:, 4 * n:4 * n + 4, :], x_in[:, 4 * n:4 * n + 4, :]).then_inc(x_landed[n], 16)
            with sp.Fori(1, PIECES // SLOTS) as m:
                for s in range(SLOTS):
                    sp.wait_ge(lo_ready[s % 2], m * 2 + (s // 2 - 1))
                    sp.dma_start(raw[:, s, :], stream[m * SLOTS + s]).then_inc(landed[s], 16)
            for g in range(PIECES // SLOTS * SLOTS, PIECES):
                sp.wait_ge(lo_ready[g % 2], g // 2 - 1)
                sp.dma_start(raw[:, g % SLOTS, :], stream[g]).then_inc(landed[g % SLOTS], 16)
            groups = ((0, 4), (4, 8), (8, 12), (12, 14), (14, 16))
            for a, b in groups:
                sp.wait_ge(x_new, 2 * XC + b)
                sp.dma_start(y_out[:, a:b, :], x[:, a:b, :]).then_inc(out_stored, 16)
            sp.wait_ge(out_stored, 16 * len(groups))
            sp.wait_ge(stored, 32 + 48 * H)
            sp.wait_ge(small_stored, 32)

        @block.tensor
        def _(pe):
            def tile_start(T, per, i):
                if i is not None or T >= 4:
                    pe.wait_ge(tile_evicted, at(T - 3, per, i))

            def piece_start(g, per, i):
                pe.wait_ge(lo_ready[g % 2], at(g // 2 + 1, per // 2, i))

            def multiply(T, g, j, k, mov_hi, mov_lo, first, last):
                out = bank[T % 4][:, 0:TOK]
                wh = whi[:, g % SLOTS, j * P:(j + 1) * P]
                wl = wlo[:, g % SLOTS, j * P:(j + 1) * P]
                pe.matmul(out, wh, mov_hi[:, k, :], start=first, stop=False)
                pe.matmul(out, wh, mov_lo[:, k, :], start=False, stop=False)
                return pe.matmul(out, wl, mov_hi[:, k, :], start=False, stop=last)

            def project(T, g, tper, gper, i, x_from=None, between=None):
                tile_start(T, tper, i)
                for n in range(XC // CH):
                    piece_start(g + n, gper, i)
                    for j in range(CH):
                        k = n * CH + j
                        if x_from is not None:
                            pe.wait_ge(x_ready, x_from + k + 1)
                        last = multiply(T, g + n, j, k, xh, xl, k == 0, k == XC - 1)
                        if j == CH - 1:
                            last.then_inc(piece_done, 1)
                        if between is not None:
                            between(k)

            def project_two(T, g, x_from):
                tile_start(T, 0, None)
                tile_start(T + 1, 0, None)
                for n in range(XC // CH):
                    for j in range(CH):
                        k = n * CH + j
                        pe.wait_ge(x_ready, x_from + k + 1)
                        for t in range(2):
                            if j == 0:
                                piece_start(g + 2 * n + t, 0, None)
                            last = multiply(T + t, g + 2 * n + t, j, k, xh, xl, k == 0, k == XC - 1)
                            if j == CH - 1:
                                last.then_inc(piece_done, 1)

            def keep_warm(n, out=bank[5]):
                for _ in range(n):
                    pe.matmul(out[:, 0:P], ones[:, :], ones[:, :], start=True, stop=True)

            def column_sums(out, src):
                pe.matmul(out, ones[:, :], src, start=True, stop=True).then_inc(norm_sum, 1)

            def down(T, g, per_tile, tiles, n_chunks, tper, gper, i, h_from):
                for f in range(tiles * n_chunks):
                    t, k = divmod(f, n_chunks)
                    if k == 0:
                        tile_start(T + t, tper, i)
                    if f % CH == 0:
                        piece_start(g + f // CH, gper, i)
                        pe.wait_ge(h_ready, h_from + min(n_chunks, k + CH))
                    last = multiply(T + t, g + f // CH, f % CH, k, hh, hl, k == 0, k == n_chunks - 1)
                    if f % CH == CH - 1:
                        last.then_inc(piece_done, 1)

            def ffn(g, T, h_from, x_from, sums):
                for half, n in enumerate(FF_HALVES):
                    start = 0
                    if half == 0:
                        project_two(T, g, x_from)
                        project(T + 2, g + 4, 0, 0, None)
                        pe.wait_ge(xsq_sum, sums)
                        column_sums(bank[4][:, 0:TOK], y[:, 0, :])
                        project(T + 3, g + 6, 0, 0, None)
                        start = 1
                    with pe.Fori(start, n // 2) as i:
                        for q in range(4):
                            project(T + q, g + 2 * q, 4, 8, i)
                    T, g = T + 2 * n, g + UP_PIECES[half]
                    tiles = 4 if half == 0 else 8
                    with pe.Fori(0, XC // tiles) as i:
                        down(T, g, 0, tiles, n, tiles, tiles * n // CH, i, h_from)
                    T, g, h_from = T + XC, g + DOWN_PIECES[half], h_from + n
                return g, T

            pe.wait_ge(consts_ready, 1)
            keep_warm(16)
            ffn(0, 0, 0, 0, 1)
            keep_warm(8)
            pe.wait_ge(ssq_added, SQ_BUFS + XC)
            column_sums(bank[4][:, 0:TOK], ssq[:, :])
            keep_warm(20)

            def square_sum(k):
                pe.wait_ge(xsq_ready, XC + k + 1)
                mm = pe.matmul(bank[4][:, 0:TOK], ones[:, :], y[:, k, :], start=(k == 0), stop=(k == XC - 1),
                               skip_group_check=True)
                if k == XC - 1:
                    mm.then_inc(norm_sum, 1)

            pe.wait_ge(norm_var, 2)
            project(GATE_T, GATE_P, 0, 0, None, XC, between=lambda k: k and square_sum(k - 1))
            square_sum(XC - 1)

            def broadcast_rows(h):
                pe.wait_ge(args_ready, 1)
                pe.wait_ge(rows_ready, 4)
                pe.wait_ge(sel_ready, at(1, 1, h))
                pe.wait_ge(tile_evicted, at(HEAD_T + 1, HEAD_TILES, h))
                pe.wait_ge(norm_var, 3)
                half = ROWS // 2
                pe.matmul(bank[5][:, 0:half], sel[:, :], rows[:, 0:half], start=True, stop=True).then_inc(rowsT_done, 1)
                pe.matmul(bank[6][:, 0:half], sel[:, :], rows[:, half:ROWS], start=True, stop=True).then_inc(rowsT_done, 1)
                I4 = ident[0:H, 0:H]
                for t in range(2):
                    pe.transpose(bank[4][:, 4 * t:4 * t + 4], rowc[:, t * P:(t + 1) * P], I4)
                    pe.transpose(bank[4][:, 8 + 4 * t:12 + 4 * t], rows[:, R_GK + t * P:R_GK + (t + 1) * P], I4)
                pe.transpose(bank[4][0:NS, 16:20], rowc[:, SEQ:TOK], I4)
                pe.transpose(bank[4][0:NS, 20:24], rows[:, R_GK + SEQ:R_GK + TOK], I4).then_inc(rowsT_done, 1)

            def to_token_major(h):
                pe.wait_ge(tile_evicted, at(HEAD_T + 8, HEAD_TILES, h))
                for j, src in enumerate((2, 1)):
                    for c in range(DC):
                        mm = pe.transpose(bank[7][0:NS, (2 * j + c) * P:(2 * j + c + 1) * P],
                                          qkvo[:, src, c, SEQ:TOK], ident[:, :])
                mm.then_inc(tr_done, 1)
                pe.wait_ge(bc_ready, at(2, 2, h))
                for b, src in ((5, 2), (6, 1)):
                    for t in range(2):
                        for c in range(DC):
                            mm = pe.transpose(bank[b][:, (2 * t + c) * P:(2 * t + c + 1) * P],
                                              qkvo[:, src, c, t * P:(t + 1) * P], ident[:, :])
                    mm.then_inc(tr_done, 1)

            def query_memory(h, b):
                if b == 0:
                    pe.wait_ge(c_landed, at(16, 16, h))
                    pe.wait_ge(qw_ready, at(1, 1, h))
                    pe.wait_ge(tr_evicted, at(2, 2, h))
                for c in range(DC):
                    mm = pe.matmul(bank[7][0:NS, 0:DH], qm[c][:, b * NS:(b + 1) * NS], C[:, b, c, :],
                                   start=(b + c == 0), stop=(b + c == NB + DC - 2), skip_group_check=True)
                if b == NB - 1:
                    mm.then_inc(qc_done, 1)

            def update_memory(h, b):
                if b >= 2:
                    pe.wait_ge(cu_evicted, at(b - 1, NB + 1, h))
                out = bank[5 + b % 2]
                for c in range(DC):
                    if b < NB:
                        mm = pe.matmul(out[:, c * DH:(c + 1) * DH], ksm[:, b, c * P:(c + 1) * P], vs[:, :],
                                       start=True, stop=True)
                    else:
                        for t in range(2):
                            mm = pe.matmul(out[:, c * DH:(c + 1) * DH], ktg[:, t, c * P:(c + 1) * P],
                                           vtok[:, t, :], start=(t == 0), stop=(t == 1))
                mm.then_inc(cu_done, 1)

            def scores(h):
                pe.wait_ge(col_ready, at(1, 1, h))
                pe.wait_ge(tile_evicted, at(HEAD_T + 10, HEAD_TILES, h))
                k, q = qkvo[:, 1, :, :], qkvo[:, 0, :, :]
                for lo, n, s, m, l in ((0, SEQ, 0, P, 0), (SEQ, P, P, P, P), (SEQ + P, NS, SEQ, NS, SEQ)):
                    for c in range(DC):
                        mm = pe.matmul(bank[4][0:m, lo:lo + n], k[:, c, s:s + m], q[:, c, l:l + n],
                                       start=(c == 0), stop=(c == DC - 1))
                mm.then_inc(sc_done, 1)

            def denominators(h):
                pe.wait_ge(st_ready, at(1, 1, h))
                pe.wait_ge(qc_evicted, at(1, 1, h))
                out = bank[7]
                pe.matmul(out[:, 0:SEQ], ones[:, :], st[:, 0:SEQ], start=True, stop=False, skip_group_check=True)
                pe.matmul(out[:, P:SEQ], ones[:, :], st[:, SEQ:SEQ + P], start=False, stop=True, skip_group_check=True)
                pe.matmul(out[:, SEQ:TOK], ones[0:NS, :], st[0:NS, SEQ + P:SEQ + P + NS],
                          start=False, stop=False, skip_group_check=True)
                for c in range(DC):
                    mm = pe.matmul(out[:, SEQ:TOK], ones[:, :], qwn[:, c, :], start=False, stop=(c == DC - 1),
                                   skip_group_check=True)
                mm.then_inc(num_done, 1)

            def attend(h):
                pe.wait_ge(cu_evicted, at(NB + 1, NB + 1, h))
                for e in range(DC):
                    out = bank[5 + e]
                    pe.matmul(out[:, 0:SEQ], vtok[:, 0, e * P:(e + 1) * P], st[:, 0:SEQ], start=True, stop=False,
                              skip_group_check=True)
                    pe.matmul(out[:, P:SEQ], vtok[:, 1, e * P:(e + 1) * P], st[:, SEQ:SEQ + P], start=False,
                              stop=True, skip_group_check=True)
                    pe.matmul(out[:, SEQ:TOK], vs[:, e * P:(e + 1) * P], st[0:NS, SEQ + P:SEQ + P + NS],
                              start=False, stop=False, skip_group_check=True)
                    pe.matmul(out[:, SEQ:TOK], qct[:, e * P:(e + 1) * P], ident[0:NS, 0:NS],
                              start=False, stop=True, skip_group_check=True).then_inc(num_done, 1)

            with pe.Fori(0, H) as h:
                def in_first_o(k):
                    if k == CH:
                        scores(h)
                    elif k > CH:
                        query_memory(h, k - CH - 1)
                    if k == XC - 1:
                        query_memory(h, NB - 1)

                def in_second_o(k):
                    if k <= NB:
                        update_memory(h, k)
                    elif k == NB + 3:
                        denominators(h)

                for q in range(HEAD_TILES):
                    project(HEAD_T + q, HEAD_P + 2 * q, HEAD_TILES, 2 * HEAD_TILES, h,
                            between=in_first_o if q == 10 else in_second_o if q == 11 else None)
                    if q == 4:
                        broadcast_rows(h)
                    if q == 8:
                        to_token_major(h)
                    if q == 11:
                        attend(h)

            def out_half(T, g, q, lo, i):
                piece_start(g, 8, i)
                for j in range(CH):
                    if lo:
                        last = multiply_conv(T, g, j)
                    else:
                        last = multiply(T, g, j, j, mh, ml, j == 0, False)
                last.then_inc(piece_done, 1)

            def multiply_conv(T, g, j):
                out = bank[T % 4][:, 0:TOK]
                wh = whi[:, g % SLOTS, j * P:(j + 1) * P]
                wl = wlo[:, g % SLOTS, j * P:(j + 1) * P]
                pe.matmul(out, wh, xh[:, j, :], start=False, stop=False)
                pe.matmul(out, wh, xh[:, CC + j, :], start=False, stop=False)
                return pe.matmul(out, wl, xh[:, j, :], start=False, stop=(j == CH - 1))

            pe.wait_ge(ysum_added, 2 * H)
            pe.wait_ge(st_ready, H)
            pe.matmul(bank[4][:, 0:TOK], ones[:, :], ysum, start=True, stop=True).then_inc(ln_sum, 1)
            tile_start(OUT_T, 0, None)
            keep_warm(14, bank[OUT_T % 4])
            pe.wait_ge(mix_ready, 2 * H)
            for q in range(4):
                tile_start(OUT_T + q, 0, None)
                out_half(OUT_T + q, OUT_P + q, q, False, None)
                if q == 1:
                    pe.wait_ge(hm_ready, 2 * H)
                    for c in range(CC):
                        pe.wait_ge(ln_sq, c + 1)
                        mm = pe.matmul(bank[5][:, 0:TOK], ones[:, :], sq8[:, c, :], start=(c == 0), stop=(c == CC - 1))
                    mm.then_inc(ln_sqsum, 1)
            for j in range(CH):
                pe.wait_ge(conv_ready, j + 1)
                for q in range(2):
                    if j == 0:
                        piece_start(OUT_P + 4 + q, 0, None)
                    last = multiply_conv(OUT_T + q, OUT_P + 4 + q, j)
            last.then_inc(piece_done, 2)
            for q in range(2, 4):
                out_half(OUT_T + q, OUT_P + 4 + q, q, True, None)
            with pe.Fori(1, XC // 4) as i:
                for q in range(4):
                    tile_start(OUT_T + q, 4, i)
                    out_half(OUT_T + q, OUT_P + q, q, False, i)
                for q in range(4):
                    out_half(OUT_T + q, OUT_P + 4 + q, q, True, i)
            keep_warm(8)
            pe.wait_ge(ssq_added, SQ_BUFS + 2 * XC)
            column_sums(bank[4][:, 0:TOK], ssq[:, :])
            keep_warm(20)
            ffn(FFN2_P, FFN2_T, sum(FF_HALVES), 2 * XC, 2)
            pe.wait_ge(ssq_added, SQ_BUFS + 3 * XC)
            column_sums(bank[4][:, 0:TOK], ssq[:, :])

        @block.scalar
        def _(act):
            def split_hi(g, per=0, i=None):
                if g >= PIECES:
                    return
                act.wait_ge(landed[g % SLOTS], at(16 * (g // SLOTS + 1), 16 * per // SLOTS, i))
                if g >= SLOTS or i is not None:
                    act.wait_ge(piece_done, at(g - 3, per, i))
                act.activation(whi[:, g % SLOTS, :], raw[:, g % SLOTS, :], ACT.Copy).then_inc(hi_ready, 1)

            def norm_root(k, scale):
                act.activation(warm[:, k:k + 1], ones[:, 0:1], ACT.Sqrt)
                act.wait_ge(norm_var, k + 1)
                act.activation(scr[:, 6, :], scr[:, 5, :], ACT.Sqrt, scale=scale).then_inc(norm_sd, 1)

            def x_operands(g, pre, n_new, splits):
                for c in range(XC):
                    for p in splits:
                        if splits[p] == c:
                            split_hi(g + p)
                    if n_new is None:
                        act.wait_ge(x_landed[c // 4], 16)
                    else:
                        act.wait_ge(x_new, n_new + c + 1)
                    act.activation(xh[:, c, :], x[:, c, :], ACT.Copy, scale=gain(pre, c)).then_inc(x_hi, 1)
                    if n_new is not None or c % 2:
                        act.activation(y[:, c, :], x[:, c, :], ACT.Square).then_inc(xsq_ready, 1)

            def ffn(g, T, f_from, sq_from, norm_at):
                for half, n in enumerate(FF_HALVES):
                    def body(i, first):
                        for jj in range(2):
                            f = f_from + jj
                            if not first:
                                split_hi(g + 4 * jj + 3, 8, i)
                                split_hi(g + 4 * jj + 4, 8, i)
                            elif jj == 0:
                                for p in range(5, 9):
                                    split_hi(g + p)
                                norm_root(norm_at, 1.0)
                            else:
                                split_hi(g + 9)
                            act.wait_ge(tile_evicted, at(T + 2 * jj + 1, 4, i))
                            if i is not None or f >= 1:
                                act.wait_ge(gated, at(f, 2, i))
                            act.activation(scr[:, 2, :], scr[:, jj, :], ACT.Sigmoid).then_inc(sig_ready, 1)
                            if not first:
                                split_hi(g + 4 * jj + 5, 8, i)
                            if not first or jj:
                                split_hi(g + 4 * jj + 6, 8, i)
                            act.wait_ge(h_f32, at(f + 1, 2, i))
                            act.activation(hh[:, jj if i is None else i * 2 + jj, :], scr[:, 4, :], ACT.Copy)\
                               .then_inc(h_hi, 1)

                    if half == 0:
                        body(None, True)
                    with act.Fori(1 - half, n // 2) as i:
                        body(i, False)
                    T, g = T + 2 * n, g + UP_PIECES[half]
                    tiles = 4 if half == 0 else 8
                    per = tiles * n // CH
                    loops = XC // tiles
                    last = g + per * loops == PIECES
                    with act.Fori(0, loops - last) as i:
                        down_body(g, T, tiles, n, per, i, half, sq_from, 0)
                    if last:
                        d = tiles * (loops - 1)
                        down_body(g + per * (loops - 1), T + d, tiles, n, per, None, half, sq_from + d, d)
                    T, g, f_from = T + XC, g + DOWN_PIECES[half], f_from + n

            def down_body(g, T, tiles, n, per, i, half, sq_from, d0):
                t = 0
                for p in range(per):
                    split_hi(g + p + LOOK, per, i)
                    if (p + 1) * CH >= (t + 1) * n:
                        if half == 1:
                            act.wait_ge(tile_evicted, at(T + t + 1, tiles, i))
                            act.wait_ge(ssq_added, at(SQ_BUFS + sq_from + t - 1, tiles, i))
                            act.activation(sq[:, (sq_from + t) % 2, :], y[:, at(d0 + t, tiles, i), :],
                                           ACT.Square).then_inc(sq_ready, 1)
                        t += 1

            act.wait_ge(vec_landed, 16)
            x_operands(0, "g_ffn1_pre", None, START_SPLITS)
            ffn(0, 0, 0, 0, 0)
            split_hi(GATE_P + 3)
            norm_root(1, 4.0)
            x_operands(GATE_P, "g_mix_pre", 0, NEXT_SPLITS)
            norm_root(2, 1.0)

            act.wait_ge(az_ready, 1)
            act.activation(scr[0:H, 3, :], scr[0:H, 2, :], ACT.Exp, scale=-1.0).then_inc(e_ready, 1)
            split_hi(HEAD_P + 3)
            act.wait_ge(e1_ready, 1)
            act.activation(scr[0:H, 4, :], scr[0:H, 3, :], ACT.Ln).then_inc(ln_ready, 1)
            split_hi(HEAD_P + 4)
            act.wait_ge(args_ready, 1)
            for k in range(2):
                act.activation(compact(rows[:, R_EM:R_EM + TOK], k), padded(mrun, k), ACT.Exp, scale=-1.0)\
                   .then_inc(rows_ready, 1)
            act.activation(rows[:, R_GK:R_GK + TOK], scr[0:H, 6, :], ACT.Exp).then_inc(rows_ready, 1)
            act.activation(rows[:, R_WI:ROWS], scr[0:H, 0, 0:NS], ACT.Exp).then_inc(rows_ready, 1)

            act.wait_ge(m_ready, 1)
            act.dma_start(m_out[:, 0:NT], mout[:, 0:NT]).then_inc(stored, 16)
            act.dma_start(m_out[:, NT:1 + NB], mout[:, NT:1 + NB]).then_inc(stored, 16)

            with act.Fori(0, H) as h:
                for q in range(HEAD_TILES):
                    if q == 0:
                        act.wait_ge(hi_ready, at(HEAD_P + 5, 2 * HEAD_TILES, h))
                        act.dma_start(hist[:, :, :], conv_in[h]).then_inc(hist_landed, 16)
                    if q in (1, 3):
                        act.wait_ge(tile_evicted, at(HEAD_T + q + 1, HEAD_TILES, h))
                        act.activation(scr[:, 2, :], scr[:, 1, :], ACT.Sigmoid).then_inc(sigb_ready, 1)
                    if q == 1:
                        act.wait_ge(hist_landed, at(16, 16, h))
                        for j in range(2):
                            act.activation(up_dec(j, HIST), hist[:, j, :].rearrange("p (b w) -> p b w", b=NB),
                                           ACT.Copy).then_inc(hist_ready, 1)
                    if q in (2, 4):
                        j = q // 2 - 1
                        act.wait_ge(u_ready, at(j + 1, 2, h))
                        act.wait_ge(stored, at(32, 48, h))
                        act.activation(newc[:, j, 0:HIST], up_prompt(j, HIST, SEQ), ACT.Copy)
                        act.activation(newc[:, j, HIST:NEW_C].rearrange("p (b w) -> p b w", b=NB),
                                       up_dec(j, HIST, NT), ACT.Copy).then_inc(newc_ready, 1)
                    if q == 3:
                        act.dma_start(C[:, :, :, :], c_in[h]).then_inc(c_landed, 16)
                    if q == 4:
                        act.wait_ge(newc_ready, at(2, 2, h))
                        act.dma_start(conv_out[h], newc[:, :, :]).then_inc(stored, 16)
                        for k in range(2):
                            act.wait_ge(rowsT_done, at(k + 1, 3, h))
                            half = ROWS // 2
                            act.activation(bc[:, k * half:(k + 1) * half], bank[5 + k][:, 0:half], ACT.Copy)\
                               .then_inc(bc_ready, 1)
                    if q == 5:
                        act.wait_ge(bc_ready, at(2, 2, h))
                        act.wait_ge(col_ready, at(1, 1, h))
                        act.activation(wt[:, 0:SEQ], bc[:, R_BM:R_BM + SEQ], ACT.Exp, bias=colc[:, 0:1])
                        act.activation(wt[:, SEQ:SEQ + P], bc[:, R_BM + P:R_BM + SEQ], ACT.Exp, bias=colc[:, 1:2])
                        act.activation(wt[0:NS, SEQ + P:SEQ + P + NS], bc[0:NS, R_BM + SEQ:R_BM + TOK], ACT.Exp,
                                       bias=cols[:, 0:1]).then_inc(w_exp, 1)
                    if q == 8:
                        act.wait_ge(tr_done, at(1, 3, h))
                        act.activation(vs[:, :], bank[7][0:NS, 0:DH], ACT.Copy)
                        act.wait_ge(gkm_ready, at(1, 1, h))
                        for b in range(NB):
                            last = act.activation(ksm[:, b, :], bank[7][0:NS, DH:2 * DH], ACT.Copy,
                                                  scale=gkm[:, b:b + 1])
                        last.then_inc(tr_evicted, 1)
                    if q == 9:
                        act.wait_ge(tr_done, at(3, 3, h))
                        act.activation(vtok[:, :, :].rearrange("p t e -> p (t e)"), bank[5][:, :], ACT.Copy)
                        for t in range(2):
                            last = act.activation(ktg[:, t, :], bank[6][:, t * DH:(t + 1) * DH], ACT.Copy,
                                                  scale=colc[:, 2 + t:3 + t])
                        last.then_inc(tr_evicted, 1)
                    if q == 11:
                        act.wait_ge(num_done, at(1, 3, h))
                        act.activation(scr[:, 2, :], bank[7][:, 0:TOK], ACT.Abs).then_inc(den_ready, 1)
                    if q in (10, 11):
                        o = q - 10
                        act.wait_ge(tile_evicted, at(HEAD_T + q + 1, HEAD_TILES, h))
                        act.activation(qkvo[:, 3, o, :], scr[:, o, :], ACT.Sigmoid).then_inc(osig_ready, 1)
                    if q == 10:
                        act.wait_ge(qc_done, at(1, 1, h))
                        act.activation(qct[:, :], bank[7][0:NS, 0:DH], ACT.Copy).then_inc(qc_evicted, 1)
                    if q == 11:
                        for e in range(DC):
                            act.wait_ge(hm_ready, at(e + 1, 2, h))
                            act.activation(mh[:, h * DC + e, :], scr[:, e, :], ACT.Copy).then_inc(hm_hi, 1)
                        act.wait_ge(cu_evicted, at(NB + 1, NB + 1, h))
                        act.dma_start(cs_out[h], C[:, :, :, :]).then_inc(stored, 16)
                        act.dma_start(cp_out[h], cpr[:, :, :]).then_inc(stored, 16)
                    split_hi(HEAD_P + 2 * q + 5, 2 * HEAD_TILES, h)
                    split_hi(HEAD_P + 2 * q + 6, 2 * HEAD_TILES, h)

            for c in range(CC):
                act.wait_ge(ln_cent, c + 1)
                act.activation(sq8[:, c, :], yc[:, c, :], ACT.Square).then_inc(ln_sq, 1)
            split_hi(OUT_P + 5)
            act.activation(warm[:, 6:7], ones[:, 0:1], ACT.Sqrt)
            act.wait_ge(ln_var, 1)
            act.activation(scr[:, 6, :], scr[:, 5, :], ACT.Sqrt).then_inc(ln_sd, 1)
            act.wait_ge(stored, 32 + 48 * H)
            for c in range(CC + 1):
                if c == 5:
                    split_hi(OUT_P + 6)
                if c < CC:
                    act.wait_ge(ln_yn, c + 1)
                    act.activation(sg8[:, c, :], yc[:, c, :], ACT.Sigmoid, scale=vec[:, V_GLN + c:V_GLN + c + 1],
                                   bias=vec[:, V_BLN + c:V_BLN + c + 1]).then_inc(ln_sig, 1)
                if c:
                    act.wait_ge(ln_silu, c)
                    act.activation(xh[:, c - 1, :], yc[:, c - 1, :], ACT.Copy).then_inc(ln_hi, 1)

            def out_body(i, i0):
                for p in range(8):
                    if i is not None or p >= 4:
                        split_hi(OUT_P + p + LOOK + 8 * i0, 8, i)
                    if p >= 4:
                        t = p - 4
                        act.wait_ge(tile_evicted, at(OUT_T + t + 1 + 4 * i0, 4, i))
                        n = XC + t + 4 * i0
                        act.wait_ge(ssq_added, at(SQ_BUFS + n - 1, 4, i))
                        act.activation(sq[:, n % 2, :], y[:, at(t + 4 * i0, 4, i), :], ACT.Square).then_inc(sq_ready, 1)

            out_body(None, 0)
            with act.Fori(1, XC // 4) as i:
                out_body(i, 0)
            split_hi(FFN2_P + 3)
            norm_root(3, 1.0)
            x_operands(FFN2_P, "g_ffn2_pre", XC, NEXT_SPLITS)
            ffn(FFN2_P, FFN2_T, sum(FF_HALVES), 2 * XC, 4)
            norm_root(5, 4.0)

        @block.vector
        def _(dve):
            chain = Chain(dve, dve_chain)
            link = chain.link

            def split_lo(g, per=0, i=None):
                if g % 2 or g >= PIECES:
                    return
                dve.wait_ge(hi_ready, at(g + 1, per, i))
                dve.tensor_tensor(wlo[:, g % SLOTS, :], raw[:, g % SLOTS, :], whi[:, g % SLOTS, :].bitcast(F32),
                                  ALU.subtract).then_inc(lo_ready[0], 1)

            def norm_factor(k, out):
                dve.wait_ge(norm_sum, k + 1)
                dve.tensor_scalar(scr[:, 5, :], bank[4][:, 0:TOK], 1.0 / D_MODEL, EPS, ALU.mult, ALU.add)\
                   .then_inc(norm_var, 1)
                dve.wait_ge(norm_sd, k + 1)
                ins = dve.reciprocal(out[:, :], scr[:, 6, :])
                if out is rpost:
                    ins.then_inc(rpost_ready, 1)
                else:
                    link(ins)

            def x_lo(pre, c, n_x):
                dve.wait_ge(x_hi, n_x + c + 1)
                dve.scalar_tensor_tensor(out=xl[:, c, :], in0=x[:, c, :], scalar=gain(pre, c),
                                         in1=xh[:, c, :].bitcast(F32), op0=ALU.mult, op1=ALU.subtract)\
                   .then_inc(x_ready, 1)

            def x_operands(g, pre, n_x, splits):
                for c in range(XC):
                    for p in splits:
                        if splits[p] == c and p < SLOTS:
                            split_lo(g + p)
                    x_lo(pre, c, n_x)
                split_lo(g + 4)

            def residual(g, post, pre, n_x, n_new):
                for c in range(XC + 1):
                    if c < XC:
                        dve.wait_ge(t_ready, n_new + c + 1)
                        dve.scalar_tensor_tensor(out=x[:, c, :], in0=scr[:, c % 4, :], scalar=gain(post, c),
                                                 in1=x[:, c, :], op0=ALU.mult, op1=ALU.add).then_inc(x_new, 1)
                    if c:
                        x_lo(pre, c - 1, n_x)
                split_lo(g + 4)

            def last_residual(post, n_new):
                dve.wait_ge(rpost_ready, 3)
                mine = range(2, XC, 3)
                theirs = 0
                for c in range(XC):
                    if c + 1 in mine:
                        if c + 1 > mine[0]:
                            dve.wait_ge(x_new, n_new + c - 1)
                        link(dve.tensor_tensor(scr[:, 4, :], y[:, c + 1, :], rpost[:, :], ALU.mult))
                    if c not in mine:
                        theirs += 1
                        dve.wait_ge(t_ready, n_new + theirs)
                    t = scr[:, 4 if c in mine else c % 4, :]
                    dve.scalar_tensor_tensor(out=x[:, c, :], in0=t, scalar=gain(post, c),
                                             in1=x[:, c, :], op0=ALU.mult, op1=ALU.add).then_inc(x_new, 1)

            def square_tree(k, g):
                dve.wait_ge(xsq_ready, k)
                n = XC // 2
                while n:
                    ins = dve.tensor_tensor(y[:, 0:n, :], y[:, 0:n, :], y[:, n:2 * n, :], ALU.add)
                    if n > 1:
                        link(ins)
                        if n == XC // 2:
                            split_lo(g)
                    else:
                        ins.then_inc(xsq_sum, 1)
                    n //= 2

            def evict_scaled(T, tper, i, out, k=None):
                src = bank[T % 4][:, 0:TOK]
                if k is None:
                    ins = dve.tensor_tensor(out, src, rstd[:, :], ALU.mult)
                else:
                    ins = dve.scalar_tensor_tensor(out=out, in0=src, scalar=k, in1=rstd[:, :], op0=ALU.mult,
                                                   op1=ALU.mult)
                ins.then_inc(tile_evicted, 1)
                dve.wait_ge(tile_evicted, at(T + 1, tper, i))

            def ffn(g, T, f_from, norm_at):
                for half, n in enumerate(FF_HALVES):
                    def body(i, first):
                        for jj in range(2):
                            f = f_from + jj
                            if not first:
                                split_lo(g + 4 * jj + 4, 8, i)
                            elif jj == 0:
                                split_lo(g + 8)
                            dve.wait_ge(piece_done, at(g + 4 * jj + 2, 8, i))
                            if first and jj == 0:
                                norm_factor(norm_at, rstd)
                            evict_scaled(T + 2 * jj, 4, i, scr[:, jj, :])
                            if not first or jj:
                                split_lo(g + 4 * jj + 6, 8, i)
                            dve.wait_ge(piece_done, at(g + 4 * jj + 4, 8, i))
                            evict_scaled(T + 2 * jj + 1, 4, i, scr[:, 3, :])
                            dve.wait_ge(gated, at(f + 1, 2, i))
                            dve.tensor_tensor(scr[:, 4, :], scr[:, 5 + jj, :], scr[:, 3, :], ALU.mult).then_inc(h_f32, 1)
                            dve.wait_ge(h_hi, at(f + 1, 2, i))
                            k = jj if i is None else i * 2 + jj
                            dve.tensor_tensor(hl[:, k, :], scr[:, 4, :], hh[:, k, :].bitcast(F32), ALU.subtract)\
                               .then_inc(h_ready, 1)
                    start = 0
                    if half == 0:
                        body(None, True)
                        start = 1
                    with dve.Fori(start, n // 2) as i:
                        body(i, False)
                    T, g = T + 2 * n, g + UP_PIECES[half]
                    tiles = 4 if half == 0 else 8
                    per = tiles * n // CH
                    loops = XC // tiles
                    with dve.Fori(0, loops if g + per * loops < PIECES else loops - 1) as i:
                        down_body(g, T, tiles, n, per, i, half, 0)
                    if g + per * loops >= PIECES:
                        down_body(g + per * (loops - 1), T + tiles * (loops - 1), tiles, n, per, None, half,
                                  tiles * (loops - 1))
                    T, g, f_from = T + XC, g + DOWN_PIECES[half], f_from + n

            def down_body(g, T, tiles, n, per, i, half, d0):
                t = 0
                for p in range(per):
                    split_lo(g + p + LOOK, per, i)
                    if (p + 1) * CH >= (t + 1) * n:
                        dve.wait_ge(piece_done, at(g + p + 1, per, i))
                        out = y[:, at(d0 + t, tiles, i), :]
                        src = bank[(T + t) % 4][:, 0:TOK]
                        if half == 0:
                            ins = dve.tensor_copy(out, src)
                        else:
                            ins = dve.tensor_tensor(out, src, out, ALU.add)
                        ins.then_inc(tile_evicted, 1)
                        t += 1

            dve.wait_ge(vec_landed, 16)
            x_operands(0, "g_ffn1_pre", 0, START_SPLITS)
            square_tree(XC, 6)
            ffn(0, 0, 0, 0)
            norm_factor(1, rpost)
            residual(GATE_P, "g_ffn1_post", "g_mix_pre", XC, 0)
            norm_factor(2, rstd)

            dve.wait_ge(piece_done, GATE_P + 2)
            g_in, g_f, g_az, g_e, g_ln, g_lf, g_arg = (scr[0:H, k, :] for k in range(7))
            gates = bank[GATE_T % 4]
            dve.tensor_tensor(g_in, gates[0:H, 0:TOK], rstd[0:H, :], ALU.mult)
            dve.tensor_tensor(g_f, gates[32:32 + H, 0:TOK], rstd[32:32 + H, :], ALU.mult).then_inc(tile_evicted, 1)
            dve.wait_ge(tile_evicted, GATE_T + 1)
            dve.wait_ge(small_landed, 32)
            dve.wait_ge(pads_ready, 2)
            dve.tensor_scalar(g_in, g_in, gv[:, 0:1], None, ALU.add)
            link(dve.tensor_scalar(g_f, g_f, gv[:, 1:2], None, ALU.add))
            dve.scalar_tensor_tensor(out=g_az, in0=g_f, scalar=-1.0, in1=g_f, op0=ALU.mult, op1=ALU.max)\
               .then_inc(az_ready, 1)
            dve.wait_ge(e_ready, 1)
            dve.tensor_scalar(g_e, g_e, 1.0, None, ALU.add).then_inc(e1_ready, 1)
            for k in range(2):
                dve.tensor_copy(padded(igp, k), compact(g_in, k))
            dve.tensor_copy(resets(igp), gv[:, 2:2 + NB].rearrange("h (b t) -> h b t", t=1))
            dve.wait_ge(ln_ready, 1)
            link(dve.scalar_tensor_tensor(out=g_lf, in0=g_f, scalar=0.0, in1=g_ln, op0=ALU.min, op1=ALU.subtract))
            for k in range(2):
                dve.tensor_copy(padded(lfb, k), compact(g_lf, k))
                last = dve.tensor_copy(padded(lfm, k), compact(g_lf, k))
            link(last)
            dve.tensor_tensor_scan(bsum[:, :], one[:, :], lfb[:, :], 0.0, ALU.mult, ALU.add)
            link(dve.tensor_tensor_scan(mrun[:, :], lfm[:, :], igp[:, :], 0.0, ALU.add, ALU.max))
            for k in range(2):
                dve.tensor_tensor(compact(rows[:, R_BM:R_BM + TOK], k), padded(bsum, k), padded(mrun, k), ALU.subtract)
                last = dve.tensor_tensor(compact(rowc[:, :], k), padded(igp, k), padded(bsum, k), ALU.subtract)
            link(last)
            dve.tensor_scalar(g_arg[:, 0:SEQ], rowc[:, 0:SEQ], rows[:, SEQ - 1:SEQ], None, ALU.add)
            bm_dec = compact(rows[:, R_BM:R_BM + TOK], 1)
            dve.tensor_tensor(compact(g_arg, 1), compact(rowc[:, :], 1),
                              bm_dec[:, :, NT - 1:NT].broadcast_to([H, NB, NT]), ALU.add)
            m0 = gv[:, 2:2 + NB].rearrange("h (b t) -> h b t", t=1)
            dve.tensor_tensor(g_in[:, 0:NS].rearrange("h (b t) -> h b t", b=NB), bm_dec,
                              m0.broadcast_to([H, NB, NT]), ALU.add).then_inc(args_ready, 1)
            dve.tensor_copy(mout[:, 0:1], mrun[:, SEQ:SEQ + 1])
            dve.tensor_copy(mout[:, 1:1 + NB].rearrange("h (b t) -> h b t", t=1),
                            padded(mrun, 1)[:, :, NT - 1:NT]).then_inc(m_ready, 1)

            def conv_taps(j, a, b):
                acc_p = scr[:, 3, 0:SEQ]
                acc_d = scr[:, 3, SEQ:TOK].rearrange("p (b t) -> p b t", b=NB)
                for k in range(a, b):
                    w = wcur[:, j, k:k + 1]
                    if k == 0:
                        dve.tensor_scalar(acc_p, up_prompt(j, SEQ), w, bcur[:, j:j + 1], ALU.mult, ALU.add)
                        ins = dve.tensor_scalar(acc_d, up_dec(j, NT), w, bcur[:, j:j + 1], ALU.mult, ALU.add)
                    else:
                        dve.scalar_tensor_tensor(out=acc_p, in0=up_prompt(j, SEQ, k), scalar=w, in1=acc_p,
                                                 op0=ALU.mult, op1=ALU.add)
                        ins = dve.scalar_tensor_tensor(out=acc_d, in0=up_dec(j, NT, k), scalar=w, in1=acc_d,
                                                       op0=ALU.mult, op1=ALU.add)
                    link(ins)

            HEAD_LINKS = 66
            with dve.Fori(0, H) as h:
                chain.enter(h, HEAD_LINKS)
                k_, v_ = qkvo[:, 1, :, :], qkvo[:, 2, :, :]
                for q in range(HEAD_TILES):
                    if q < 11:
                        split_lo(HEAD_P + 2 * q + 4, 2 * HEAD_TILES, h)
                    if q < 10:
                        dve.wait_ge(piece_done, at(HEAD_P + 2 * q + 2, 2 * HEAD_TILES, h))
                    T = HEAD_T + q
                    if q == 0:
                        dve.wait_ge(rows_ready, 4)
                        evict_scaled(T, HEAD_TILES, h, scr[:, 0, :])
                        dve.tensor_copy(wcur[:, :, :].rearrange("p c t -> p (c t)"),
                                        vec[:, bass.ds(h * (2 * TAPS) + V_TAP, 2 * TAPS)])
                        dve.tensor_copy(bcur[:, :], vec[:, bass.ds(h * 2 + V_BDW, 2)])
                        dve.tensor_scalar(sel[:, :], ones[0:H, :], ident[0:H, bass.ds(h, 1)], None,
                                          ALU.mult).then_inc(sel_ready, 1)
                        dve.wait_ge(sel_ready, at(1, 1, h))
                    elif q == 1:
                        evict_scaled(T, HEAD_TILES, h, scr[:, 1, :])
                    elif q == 2:
                        dve.wait_ge(u_ready, at(1, 2, h))
                        evict_scaled(T, HEAD_TILES, h, scr[:, 0, :])
                        conv_taps(0, 0, 8)
                    elif q == 3:
                        evict_scaled(T, HEAD_TILES, h, scr[:, 1, :])
                        conv_taps(0, 8, 16)
                    elif q in (4, 5):
                        evict_scaled(T, HEAD_TILES, h, k_[:, q - 4, :], DH ** -0.5)
                        conv_taps(0, 16 + 8 * (q - 4), min(24 + 8 * (q - 4), TAPS))
                        if q == 4:
                            dve.wait_ge(rowsT_done, at(3, 3, h))
                            dve.tensor_copy(colc[:, :].rearrange("p (k o) -> p k o", o=1),
                                            bank[4][:, 0:4 * H].rearrange("p (k h) -> p k h", h=H)[:, :, bass.ds(h, 1)])
                            dve.tensor_copy(cols[:, :].rearrange("p (k o) -> p k o", o=1),
                                            bank[4][0:NS, 4 * H:6 * H].rearrange("p (k h) -> p k h", h=H)
                                            [:, :, bass.ds(h, 1)]).then_inc(col_ready, 1)
                            dve.wait_ge(col_ready, at(1, 1, h))
                            dve.tensor_scalar(gkm[:, :], mask[:, :], cols[:, 1:2], None, ALU.mult)\
                                .then_inc(gkm_ready, 1)
                        else:
                            dve.tensor_copy(yc[:, h * 2, :], scr[:, 3, :]).then_inc(conv_done, 1)
                            dve.wait_ge(conv_done, at(1, 2, h))
                    elif q in (6, 7):
                        evict_scaled(T, HEAD_TILES, h, v_[:, q - 6, :])
                        dve.wait_ge(u_ready, at(2, 2, h))
                        conv_taps(1, 8 * (q - 6), 8 * (q - 5))
                    elif q in (8, 9):
                        evict_scaled(T, HEAD_TILES, h, qkvo[:, 0, q - 8, :])
                        if q == 8:
                            conv_taps(1, 16, 20)
                        else:
                            dve.wait_ge(bc_ready, at(2, 2, h))
                            wi = bc[:, R_WI:ROWS].rearrange("p (b t) -> p b t", b=NB)
                            for c in range(DC):
                                last = dve.tensor_tensor(
                                    qw[c], qkvo[:, 0, c, SEQ:TOK].rearrange("p (b t) -> p b t", b=NB), wi, ALU.mult)
                            link(last)
                            for c in range(DC):
                                last = dve.tensor_tensor(
                                    qwn[:, c, :].rearrange("p (b t) -> p b t", b=NB),
                                    qw[c],
                                    n0[:, bass.ds(h, 1), c, :].rearrange("p o b -> p b o").broadcast_to([P, NB, NT]),
                                    ALU.mult)
                            last.then_inc(qw_ready, 1)
                            conv_taps(1, 20, TAPS)
                            dve.tensor_copy(yc[:, h * 2 + 1, :], scr[:, 3, :]).then_inc(conv_done, 1)
                            dve.wait_ge(conv_done, at(2, 2, h))
                    elif q == 10:
                        dve.wait_ge(sc_done, at(1, 1, h))
                        dve.wait_ge(w_ready, at(1, 1, h))
                        n = SEQ + P
                        dve.tensor_tensor(st[:, 0:n], bank[4][:, 0:n], wt[:, 0:n], ALU.mult)
                        dve.tensor_tensor(st[0:NS, n:n + NS], bank[4][0:NS, n:n + NS], wt[0:NS, n:n + NS],
                                          ALU.mult).then_inc(st_ready, 1)
                        dve.wait_ge(piece_done, at(HEAD_P + 2 * q + 2, 2 * HEAD_TILES, h))
                        evict_scaled(T, HEAD_TILES, h, scr[:, 0, :])
                        for b in range(NB + 1):
                            dve.wait_ge(cu_done, at(b + 1, NB + 1, h))
                            src = bank[5 + b % 2][:, :]
                            if b < NB:
                                Cb = C[:, b, :, :].rearrange("p c e -> p (c e)")
                                g_st = bc[:, R_WI + b * NT + NT - 1:R_WI + (b + 1) * NT]
                                dve.scalar_tensor_tensor(out=Cb, in0=Cb, scalar=g_st, in1=src, op0=ALU.mult,
                                                         op1=ALU.add).then_inc(cu_evicted, 1)
                            else:
                                dve.wait_ge(stored, at(48, 48, h))
                                dve.tensor_copy(cpr[:, :, :].rearrange("p c e -> p (c e)"), src)\
                                   .then_inc(cu_evicted, 1)
                        split_lo(HEAD_P + 2 * q + 6, 2 * HEAD_TILES, h)
                    else:
                        dve.wait_ge(den_ready, at(1, 1, h))
                        link(dve.tensor_tensor(scr[:, 2, :], scr[:, 2, :], bc[:, R_EM:R_EM + TOK], ALU.max))
                        dve.reciprocal(scr[:, 2, :], scr[:, 2, :]).then_inc(rden_ready, 1)
                        dve.wait_ge(piece_done, at(HEAD_P + 2 * q + 2, 2 * HEAD_TILES, h))
                        evict_scaled(T, HEAD_TILES, h, scr[:, 1, :])
                        for e in range(DC):
                            dve.wait_ge(num_done, at(e + 2, 3, h))
                            dve.wait_ge(ro_ready, at(e + 1, 2, h))
                            dve.tensor_tensor(scr[:, e, :], bank[5 + e][:, 0:TOK], qkvo[:, 3, e, :], ALU.mult)\
                                .then_inc(hm_ready, 1)
                        dve.wait_ge(kg_ready, at(1, 1, h))
                        dve.tensor_reduce(nnp[:, bass.ds(h, 1), :].rearrange("p o c -> p (o c)"),
                                          scr[:, 5:7, 0:SEQ], AX_X, ALU.add)
                        link(dve.tensor_reduce(nred[:, :, :].rearrange("p c b -> p (c b)"),
                                               scr[:, 5:7, SEQ:TOK].rearrange("p c (b t) -> p c b t", b=NB), AX_X,
                                               ALU.add))
                        g_st = bc[:, R_WI:ROWS].rearrange("p (b t) -> p b t", b=NB)[:, :, NT - 1:NT]
                        for c in range(DC):
                            last = dve.tensor_tensor(scr[:, 3, c * NB:(c + 1) * NB],
                                                     n0[:, bass.ds(h, 1), c, :].rearrange("p o b -> p (o b)"),
                                                     g_st.rearrange("p b t -> p (b t)"), ALU.mult)
                        link(last)
                        dve.tensor_tensor(nns[:, bass.ds(h, 1), :, :].rearrange("p o c b -> p (o c b)"),
                                          scr[:, 3, 0:DC * NB], nred[:, :, :].rearrange("p c b -> p (c b)"), ALU.add)\
                           .then_inc(nn_ready, 1)
                        dve.wait_ge(nn_ready, at(1, 1, h))
                        for e in range(DC):
                            dve.wait_ge(hm_hi, at(e + 1, 2, h))
                            dve.tensor_tensor(ml[:, h * DC + e, :], scr[:, e, :],
                                              mh[:, h * DC + e, :].bitcast(F32), ALU.subtract).then_inc(mix_ready, 1)
                        dve.wait_ge(mix_ready, at(2, 2, h))
            chain.leave(H)

            dve.wait_ge(ln_sum, 1)
            link(dve.tensor_scalar(scr[:, 3, :], bank[4][:, 0:TOK], 1.0 / D_CONV, None, ALU.mult))
            for c in range(CC):
                dve.tensor_tensor(yc[:, c, :], yc[:, c, :], scr[:, 3, :], ALU.subtract).then_inc(ln_cent, 1)
            split_lo(OUT_P + 4)
            dve.wait_ge(ln_sqsum, 1)
            dve.tensor_scalar(scr[:, 5, :], bank[5][:, 0:TOK], 1.0 / D_CONV, EPS, ALU.mult, ALU.add)\
               .then_inc(ln_var, 1)
            dve.wait_ge(ln_sd, 1)
            link(dve.reciprocal(scr[:, 4, :], scr[:, 6, :]))
            for c in range(CC + 2):
                if c == 6:
                    split_lo(OUT_P + 6)
                if c < CC:
                    dve.tensor_tensor(yc[:, c, :], yc[:, c, :], scr[:, 4, :], ALU.mult).then_inc(ln_yn, 1)
                    dve.wait_ge(ln_yn, c + 1)
                    dve.tensor_scalar(sq8[:, c, :], yc[:, c, :], vec[:, V_GLN + c:V_GLN + c + 1],
                                      vec[:, V_BLN + c:V_BLN + c + 1], ALU.mult, ALU.add).then_inc(ln_z, 1)
                if c >= 2:
                    k = c - 2
                    dve.wait_ge(ln_hi, k + 1)
                    dve.tensor_tensor(xh[:, CC + k, :], yc[:, k, :], xh[:, k, :].bitcast(F32), ALU.subtract)\
                       .then_inc(conv_ready, 1)

            def out_body(i):
                for p in range(8):
                    if i is not None or p >= 4:
                        split_lo(OUT_P + p + LOOK, 8, i)
                    if p >= 4:
                        t = p - 4
                        dve.wait_ge(piece_done, at(OUT_P + p + 1, 8, i))
                        dve.tensor_copy(y[:, at(t, 4, i), :], bank[(OUT_T + t) % 4][:, 0:TOK]).then_inc(tile_evicted, 1)

            dve.wait_ge(stored, 32 + 48 * H)
            out_body(None)
            with dve.Fori(1, XC // 4) as i:
                out_body(i)
            norm_factor(3, rpost)
            residual(FFN2_P, "g_mix_post", "g_ffn2_pre", 2 * XC, XC)
            square_tree(3 * XC, FFN2_P + 6)
            dve.wait_ge(small_stored, 32)
            ffn(FFN2_P, FFN2_T, sum(FF_HALVES), 4)
            norm_factor(5, rpost)
            last_residual("g_ffn2_post", 2 * XC)

        @block.gpsimd
        def _(pool):
            def split_lo(g, per=0, i=None):
                if g % 2 == 0 or g >= PIECES:
                    return
                pool.wait_ge(hi_ready, at(g + 1, per, i))
                pool.tensor_tensor(wlo[:, g % SLOTS, :], raw[:, g % SLOTS, :], whi[:, g % SLOTS, :].bitcast(F32),
                                   ALU.subtract).then_inc(lo_ready[1], 1)

            def clear_ssq(k):
                if k:
                    pool.wait_ge(norm_sum, 2 * k)
                pool.memset(ssq[:, :], 0.0).then_inc(ssq_clear, 1)
                pool.wait_ge(ssq_clear, k + 1)

            def add_sq(n, per=0, i=None):
                pool.wait_ge(sq_ready, at(n + 1, per, i))
                pool.tensor_tensor(ssq[:, :], ssq[:, :], sq[:, n % 2, :], ALU.add).then_inc(ssq_added, 1)
                pool.wait_ge(ssq_added, at(SQ_BUFS + n + 1, per, i))

            def times_rpost(n_new, c):
                if n_new + c >= 4:
                    pool.wait_ge(x_new, n_new + c - 3)
                pool.tensor_tensor(scr[:, c % 4, :], y[:, c, :], rpost[:, :], ALU.mult).then_inc(t_ready, 1)

            def residual(k, n_new):
                pool.wait_ge(rpost_ready, k + 1)
                for c in range(XC):
                    times_rpost(n_new, c)

            def ffn(g, T, f_from, sq_from, k):
                for half, n in enumerate(FF_HALVES):
                    def body(i, first):
                        for jj in range(2):
                            f = f_from + jj
                            if not first:
                                split_lo(g + 4 * jj + 3, 8, i)
                            elif jj == 0:
                                split_lo(g + 5)
                                split_lo(g + 7)
                            else:
                                split_lo(g + 9)
                            pool.wait_ge(sig_ready, at(f + 1, 2, i))
                            pool.tensor_tensor(scr[:, 5 + jj, :], scr[:, jj, :], scr[:, 2, :], ALU.mult).then_inc(gated, 1)
                            if not first:
                                split_lo(g + 4 * jj + 5, 8, i)

                    if half == 0:
                        body(None, True)
                    with pool.Fori(1 - half, n // 2) as i:
                        body(i, False)
                    T, g = T + 2 * n, g + UP_PIECES[half]
                    tiles = 4 if half == 0 else 8
                    per = tiles * n // CH
                    loops = XC // tiles
                    if half == 0:
                        clear_ssq(k)
                    with pool.Fori(0, loops if g + per * loops < PIECES else loops - 1) as i:
                        down_body(g, tiles, n, per, i, half, sq_from)
                    if g + per * loops >= PIECES:
                        down_body(g + per * (loops - 1), tiles, n, per, None, half, sq_from + tiles * (loops - 1))
                    T, g, f_from = T + XC, g + DOWN_PIECES[half], f_from + n

            def down_body(g, tiles, n, per, i, half, sq_from):
                t = 0
                for p in range(per):
                    split_lo(g + p + LOOK, per, i)
                    if (p + 1) * CH >= (t + 1) * n:
                        if half == 1:
                            add_sq(sq_from + t, tiles, i)
                        t += 1

            pool.memset(ident[:, :], 0.0).then_inc(pool_chain, 1)
            pool.memset(ones[:, :], 1.0).then_inc(ssq_added, SQ_BUFS)
            pool.wait_ge(pool_chain, 1)
            pool.affine_select(out=ident[:, :], in_=ident[:, :], compare_op=ALU.not_equal, fill=1.0, base=0,
                               pattern=[[-1, P]], channel_multiplier=1).then_inc(consts_ready, 1)
            for c in range(XC):
                for p in START_SPLITS:
                    if START_SPLITS[p] == c:
                        split_lo(p)
                if c % 2 == 0:
                    pool.wait_ge(x_landed[c // 4], 16)
                    pool.tensor_tensor(y[:, c, :], x[:, c, :], x[:, c, :], ALU.mult).then_inc(xsq_ready, 1)
            ffn(0, 0, 0, 0, 0)
            split_lo(GATE_P + 3)
            residual(0, 0)
            pool.dma_start(gv[:, :], gate_vec).then_inc(small_landed, 16)
            pool.dma_start(n0[:, :, :, :], n_in).then_inc(small_landed, 16)
            pool.memset(lfb[:, :], 0.0)
            pool.memset(lfm[:, :], -3.0e38)
            pool.memset(igp[:, :], 0.0)
            pool.memset(mask[:, :], 1.0)
            pool.memset(one[:, :], 1.0).then_inc(pads_ready, 1)
            pool.wait_ge(pads_ready, 1)
            pool.memset(resets(one), 0.0)
            pool.memset(one[:, 0:1], 0.0)
            for j in range(2):
                pool.memset(up_prompt(j, HIST), 0.0)
            pool.affine_select(out=mask[:, :], in_=mask[:, :], compare_op=ALU.is_ge, fill=0.0, base=0,
                               pattern=[[-NT, NB]], channel_multiplier=1).then_inc(pool_chain, 1)
            pool.wait_ge(pool_chain, 2)
            pool.affine_select(out=mask[:, :], in_=mask[:, :], compare_op=ALU.is_ge, fill=0.0, base=NT - 1,
                               pattern=[[NT, NB]], channel_multiplier=-1).then_inc(pads_ready, 1)
            pool.wait_ge(x_new, XC)
            pool.memset(ysum, 0.0)
            for q in qm:
                pool.memset(q, 0.0)
            clear_ssq(1)
            split_lo(HEAD_P + 3)

            with pool.Fori(0, H) as h:
                for q in range(HEAD_TILES):
                    if q in (1, 3):
                        j = q // 2
                        pool.wait_ge(sigb_ready, at(j + 1, 2, h))
                        pool.wait_ge(hist_ready, at(2, 2, h))
                        pool.tensor_tensor(up_prompt(j, SEQ, HIST), scr[:, 0, 0:SEQ], scr[:, 2, 0:SEQ], ALU.mult)
                        pool.tensor_tensor(up_dec(j, NT, HIST),
                                           scr[:, 0, SEQ:TOK].rearrange("p (b t) -> p b t", b=NB),
                                           scr[:, 2, SEQ:TOK].rearrange("p (b t) -> p b t", b=NB), ALU.mult)\
                            .then_inc(u_ready, 1)
                    if q == 6:
                        pool.wait_ge(w_exp, at(1, 1, h))
                        pool.wait_ge(tile_evicted, at(HEAD_T + 6, HEAD_TILES, h))
                        pool.wait_ge(bc_ready, at(2, 2, h))
                        pool.tensor_tensor(scr[:, 5, :], qkvo[:, 1, 0, :], bc[:, R_GK:R_GK + TOK], ALU.mult)
                        diag = wt[:, 0:2 * SEQ - P].rearrange("p (k l) -> p k l", l=P)[:, 0:3:2, :]
                        pool.affine_select(out=diag, in_=diag, compare_op=ALU.is_ge, fill=0.0, base=0,
                                           pattern=[[0, 2], [1, P]], channel_multiplier=-1)
                        dec = wt[0:NS, SEQ + P:SEQ + P + NS].rearrange("p (b t) -> p b t", b=NB)
                        pool.affine_select(out=dec, in_=dec, compare_op=ALU.is_ge, fill=0.0, base=0,
                                           pattern=[[NT, NB], [1, NT]], channel_multiplier=-1).then_inc(pool_chain, 1)
                        pool.wait_ge(pool_chain, at(3, 1, h))
                        pool.tensor_tensor(scr[:, 6, :], qkvo[:, 1, 1, :], bc[:, R_GK:R_GK + TOK], ALU.mult)\
                            .then_inc(kg_ready, 1)
                        pool.affine_select(out=dec, in_=dec, compare_op=ALU.is_ge, fill=0.0, base=0,
                                           pattern=[[-NT, NB], [0, NT]], channel_multiplier=1).then_inc(w_ready, 1)
                    if q in (6, 11):
                        j = 0 if q == 6 else 1
                        pool.wait_ge(conv_done, at(j + 1, 2, h))
                        pool.tensor_tensor(ysum, ysum, yc[:, h * 2 + j, :], ALU.add).then_inc(ysum_added, 1)
                        pool.wait_ge(ysum_added, at(j + 1, 2, h))
                    if q == 11:
                        pool.wait_ge(rden_ready, at(1, 1, h))
                        for e in range(DC):
                            pool.wait_ge(osig_ready, at(e + 1, 2, h))
                            pool.tensor_tensor(qkvo[:, 3, e, :], qkvo[:, 3, e, :], scr[:, 2, :], ALU.mult)\
                                .then_inc(ro_ready, 1)
                    split_lo(HEAD_P + 2 * q + 5, 2 * HEAD_TILES, h)

            pool.wait_ge(nn_ready, H)
            pool.dma_start(ns_out, nns[:, :, :, :]).then_inc(small_stored, 16)
            pool.dma_start(np_out, nnp[:, :, :]).then_inc(small_stored, 16)
            split_lo(OUT_P + 5)
            for c in range(CC):
                pool.wait_ge(ln_sig, c + 1)
                pool.wait_ge(ln_z, c + 1)
                pool.tensor_tensor(yc[:, c, :], sq8[:, c, :], sg8[:, c, :], ALU.mult).then_inc(ln_silu, 1)

            def out_body(i):
                for p in range(8):
                    if i is not None or p >= 4:
                        split_lo(OUT_P + p + LOOK, 8, i)
                    if p >= 4:
                        add_sq(XC + p - 4, 4, i)

            out_body(None)
            with pool.Fori(1, XC // 4) as i:
                out_body(i)
            split_lo(FFN2_P + 3)
            residual(1, XC)
            ffn(FFN2_P, FFN2_T, sum(FF_HALVES), 2 * XC, 2)
            pool.wait_ge(rpost_ready, 3)
            for c in range(XC):
                if c % 3 != 2:
                    times_rpost(2 * XC, c)


def _pieces(w, order):
    chunks = w.reshape(w.shape[0] // P, P, w.shape[1] // P, P)
    flat = np.array(order).reshape(-1, CH, 2)
    out = chunks[flat[:, :, 1], :, flat[:, :, 0], :]
    return np.ascontiguousarray(out.transpose(0, 2, 1, 3)).reshape(len(flat), P, PIECE)


def _ffn_pieces(gate, up, down):
    parts, f0 = [], 0
    gu = np.concatenate([gate, up], axis=1)
    up_tile = D_FF // P
    for n in FF_HALVES:
        gate_up = _pieces(gu, [(t, k) for f in range(f0, f0 + n) for t in (f, up_tile + f) for k in range(XC)])
        if f0 == 0:
            gate_up[[1, 2]] = gate_up[[2, 1]]
        parts.append(gate_up)
        parts.append(_pieces(down, [(t, f0 + k) for t in range(XC) for k in range(n)]))
        f0 += n
    return parts


def _feature_major(a):
    return a.T.reshape(-1, P, a.shape[0]).transpose(1, 0, 2)


def kernel(**inputs):
    import concourse.bacc as bacc
    from concourse.bass_utils import run_bass_kernel_spmd

    a = {k: np.asarray(v) for k, v in inputs.items()}
    w_in = a["w_in"][0]
    gates = np.zeros((D_MODEL, P), np.float32)
    gates[:, 0:H] = w_in[:, 6 * D_MLSTM:6 * D_MLSTM + H]
    gates[:, 32:32 + H] = w_in[:, 6 * D_MLSTM + H:]
    per = D_MLSTM // P
    q0, k0, v0, o0, a0, b0 = (n * per for n in range(6))
    tiles = []
    for h in range(H):
        for c in range(2):
            tiles += [a0 + 2 * h + c, b0 + 2 * h + c]
        for base in (k0, v0, q0, o0):
            tiles += [base + DC * h, base + DC * h + 1]
    out_order = [(4 * g + q, half * CH + k) for g in range(XC // 4) for half in range(2) for q in range(4)
                 for k in range(CH)]
    stream = np.concatenate(
        _ffn_pieces(a["w_ffn1_gate"][0], a["w_ffn1_up"][0], a["w_ffn1_down"][0])
        + [_pieces(gates, [(0, k) for k in range(XC)]),
           _pieces(w_in[:, :6 * D_MLSTM], [(t, k) for t in tiles for k in range(XC)]),
           _pieces(a["w_out"][0], out_order)]
        + _ffn_pieces(a["w_ffn2_gate"][0], a["w_ffn2_up"][0], a["w_ffn2_down"][0]))
    assert len(stream) == PIECES
    col = lambda v: v.reshape(-1, P).T
    vecs = np.concatenate(
        [col(a[g][0]) for g in GAINS]
        + [a["w_dw"][0].T.reshape(CC, P, TAPS).transpose(1, 0, 2).reshape(P, CC * TAPS)]
        + [col(a[g][0]) for g in ("b_dw", "g_conv_ln", "b_conv_ln")], axis=1)
    x_in = np.concatenate([_feature_major(a["x_prompt"][0]), _feature_major(a["x_sample"].reshape(NS, D_MODEL))], axis=2)
    gate_vec = np.concatenate([a["b_igate"].T, a["b_fgate"].T, a["state_mlstm_m"][0].T], axis=1)
    c_in = a["state_mlstm_C"][0].reshape(NB, H, DC, P, DH).transpose(1, 3, 0, 2, 4)
    n_in = a["state_mlstm_n"][0].reshape(NB, H, DC, P).transpose(3, 1, 2, 0)
    conv_in = a["state_conv"][0].transpose(2, 0, 1).reshape(H, 2, P, NB * HIST).transpose(0, 2, 1, 3)
    arrays = {"stream": stream, "x_in": x_in, "vecs": vecs, "gate_vec": gate_vec, "c_in": c_in, "n_in": n_in,
              "conv_in": conv_in}
    arrays = {k: np.ascontiguousarray(v) for k, v in arrays.items()}
    outs = {"y_out": (P, XC, TOK), "cp_out": (H, P, DC, DH), "np_out": (P, H, DC), "cs_out": (H, P, NB, DC, DH),
            "ns_out": (P, H, DC, NB), "m_out": (H, 1 + NB), "conv_out": (H, P, 2, NEW_C)}

    nc = bacc.Bacc("TRN2", target_bir_lowering=False, num_devices=1)
    args = {k: nc.dram_tensor(k, v.shape, F32, kind="ExternalInput").ap() for k, v in arrays.items()}
    args |= {k: nc.dram_tensor(k, s, F32, kind="ExternalOutput").ap() for k, s in outs.items()}
    hybrid_layer_kernel(nc, **args)
    r = run_bass_kernel_spmd(nc, [arrays], core_ids=[0]).results[0]

    y = r["y_out"].transpose(2, 1, 0).reshape(TOK, D_MODEL)
    conv = r["conv_out"].transpose(3, 0, 2, 1).reshape(NEW_C, D_CONV)
    return (y[:SEQ].reshape(1, SEQ, D_MODEL), y[SEQ:].reshape(NB, NT, D_MODEL),
            r["cp_out"].transpose(0, 2, 1, 3).reshape(1, 1, H, DH, DH),
            r["np_out"].transpose(1, 2, 0).reshape(1, 1, H, DH),
            r["m_out"][:, 0].reshape(1, 1, H),
            conv[:HIST].reshape(1, 1, HIST, D_CONV),
            r["cs_out"].transpose(2, 0, 3, 1, 4).reshape(1, NB, H, DH, DH),
            r["ns_out"].transpose(3, 1, 2, 0).reshape(1, NB, H, DH),
            r["m_out"][:, 1:].T.reshape(1, NB, H),
            conv[HIST:].reshape(NB, HIST, D_CONV)[None])
```
